# Optimizing a Trainium2 kernel written in Bass

```python
import jax
import jax.numpy as jnp
from jax import lax
import numpy as np
import jax, jax.numpy as jnp

D_MODEL = 1024
BATCH = 1
SEQ = 256
DEPTH = 2

GRID_W = 64
CTX_LEN = 256
NORM_EPS = 1e-6

MLA_HEADS = 8
MLA_Q_RANK = 256
MLA_KV_RANK = 128
MLA_NOPE = 64
MLA_ROPE = 32
MLA_V = 64
MLA_WIDTH = MLA_HEADS * MLA_V
ROPE_BASE = 10000.0
Q_BLOCK = 128

POOL_WINDOWS = (2, 4, 8, 16)
POOL_WIDTH = 512
POOL_GROUP = POOL_WIDTH // len(POOL_WINDOWS)

GLA_HEADS = 4
GLA_DK = 64
GLA_DV = 128
GLA_KW = GLA_HEADS * GLA_DK
GLA_WIDTH = GLA_HEADS * GLA_DV
GLA_GATE_RANK = 16
GLA_TAU = 16.0
GLA_CHUNK = 64

N_BRANCH = 3

IN_NAMES = ('mla_q', 'mla_kv', 'mla_kr', 'mla_gate', 'pool_x', 'pool_gate',
            'gla_q', 'gla_k', 'gla_v', 'gla_af', 'gla_ab', 'gla_gate', 'merge')
IN_SIZES = (MLA_Q_RANK, MLA_KV_RANK, MLA_ROPE, MLA_WIDTH, POOL_WIDTH, POOL_WIDTH,
            GLA_KW, GLA_KW, GLA_WIDTH, GLA_GATE_RANK, GLA_GATE_RANK, GLA_WIDTH, N_BRANCH * D_MODEL)
D_IN = sum(IN_SIZES)


def rmsnorm(x, g):
    xf = x.astype(jnp.float32)
    y = xf * lax.rsqrt(jnp.mean(xf * xf, axis=-1, keepdims=True) + NORM_EPS)
    return (y * g.astype(jnp.float32)).astype(x.dtype)

def split_columns(z):
    offsets = [int(o) for o in np.cumsum(IN_SIZES)[:-1]]
    return dict(zip(IN_NAMES, jnp.split(z, offsets, axis=-1)))

def flip(t):
    return t[:, ::-1]

def axial_rope_tables(row, col):
    half = MLA_ROPE // 2
    inv = ROPE_BASE ** (-jnp.arange(0, half, 2, dtype=jnp.float32) / half)
    ang_r = row.astype(jnp.float32)[:, None] * inv
    ang_c = col.astype(jnp.float32)[:, None] * inv
    ang = jnp.concatenate([ang_r, ang_r, ang_c, ang_c], axis=-1)
    return jnp.cos(ang), jnp.sin(ang)

def apply_rope(x, cos, sin):
    half = MLA_ROPE // 2
    quarter = half // 2

    def rot(v):
        return jnp.concatenate([-v[..., quarter:], v[..., :quarter]], axis=-1)

    rotated = jnp.concatenate([rot(x[..., :half]), rot(x[..., half:])], axis=-1)
    return (x * cos + rotated * sin).astype(x.dtype)

def softmax_attention(q, k, v, scale):
    s = jnp.einsum('bqhd,bkhd->bhqk', q, k).astype(jnp.float32) * scale
    p = jax.nn.softmax(s, axis=-1).astype(v.dtype)
    return jnp.einsum('bhqk,bkhd->bqhd', p, v)

def blocked_attention(q, k, v, scale):
    B, L, H, dk = q.shape
    nblk = L // Q_BLOCK
    qb = q.reshape(B, nblk, Q_BLOCK, H, dk).transpose(1, 0, 2, 3, 4)
    ob = lax.map(lambda qq: softmax_attention(qq, k, v, scale), qb)
    return ob.transpose(1, 0, 2, 3, 4).reshape(B, L, H, v.shape[-1])

def mla_queries(zz, q_norm, w_uq):
    B, L, _ = zz['mla_q'].shape
    q = (rmsnorm(zz['mla_q'], q_norm) @ w_uq).reshape(B, L, MLA_HEADS, MLA_NOPE + MLA_ROPE)
    return q[..., :MLA_NOPE], q[..., MLA_NOPE:]

def mla_keys_values(zz, kv_norm, w_ukv):
    B, L, _ = zz['mla_kv'].shape
    kv = (rmsnorm(zz['mla_kv'], kv_norm) @ w_ukv).reshape(B, L, MLA_HEADS, MLA_NOPE + MLA_V)
    return kv[..., :MLA_NOPE], kv[..., MLA_NOPE:]

def assemble_keys(k_nope, k_rope):
    B, L, H, _ = k_nope.shape
    return jnp.concatenate([k_nope, jnp.broadcast_to(k_rope[:, :, None, :], (B, L, H, MLA_ROPE))], axis=-1)

def mla_branch(z, zc, cos, sin, q_norm, w_uq, kv_norm, w_ukv, with_ctx_out):
    B, L, _ = z['mla_q'].shape
    scale = (MLA_NOPE + MLA_ROPE) ** -0.5
    q_nope, q_rope = mla_queries(z, q_norm, w_uq)
    q = jnp.concatenate([q_nope, apply_rope(q_rope, cos[:, None, :], sin[:, None, :])], axis=-1)
    k_nope, v = mla_keys_values(z, kv_norm, w_ukv)
    k = assemble_keys(k_nope, apply_rope(z['mla_kr'], cos, sin))
    kc_nope, vc = mla_keys_values(zc, kv_norm, w_ukv)
    kc = assemble_keys(kc_nope, zc['mla_kr'])
    k_all = jnp.concatenate([kc, k], axis=1)
    v_all = jnp.concatenate([vc, v], axis=1)
    y = blocked_attention(q, k_all, v_all, scale).reshape(B, L, MLA_WIDTH)
    y = y * jax.nn.silu(z['mla_gate'])
    if with_ctx_out:
        Bc, Lc, _ = zc['mla_q'].shape
        qc = jnp.concatenate(mla_queries(zc, q_norm, w_uq), axis=-1)
        yc = softmax_attention(qc, kc, vc, scale).reshape(Bc, Lc, MLA_WIDTH) * jax.nn.silu(zc['mla_gate'])
    else:
        yc = None
    return y, yc

def multiscale_pool(u):
    B, L, W = u.shape
    uf = u.astype(jnp.float32)
    csum = jnp.concatenate([jnp.zeros((B, 1, W), jnp.float32), jnp.cumsum(uf, axis=1)], axis=1)
    t = jnp.arange(L)
    outs = []
    for g, w in enumerate(POOL_WINDOWS):
        lo = jnp.clip(t - w // 2, 0, L)
        hi = jnp.clip(t + w // 2, 0, L)
        cs = csum[..., g * POOL_GROUP:(g + 1) * POOL_GROUP]
        count = (hi - lo).astype(jnp.float32)[None, :, None]
        outs.append((jnp.take(cs, hi, axis=1) - jnp.take(cs, lo, axis=1)) / count)
    return (jnp.concatenate(outs, axis=-1) - uf).astype(u.dtype)

def pool_branch(zz, pool_w, pool_scale):
    B, L, _ = zz['pool_x'].shape
    pooled = multiscale_pool(zz['pool_x']).reshape(B, L, len(POOL_WINDOWS), POOL_GROUP)
    mixed = jnp.einsum('blgi,gio->blgo', pooled, pool_w).reshape(B, L, POOL_WIDTH)
    return mixed * pool_scale * jax.nn.silu(zz['pool_gate'])

def gla_scan(q, k, v, log_a, s0, with_out):
    B, L, H, _ = q.shape
    n = L // GLA_CHUNK

    def to_chunks(t):
        return t.reshape(B, n, GLA_CHUNK, H, t.shape[-1]).transpose(1, 0, 3, 2, 4)

    mask = jnp.tril(jnp.ones((GLA_CHUNK, GLA_CHUNK), bool))[:, :, None]

    def step(s, inp):
        qq, kk, vv, aa = inp
        b = jnp.cumsum(aa, axis=2)
        b_last = b[:, :, -1:, :]
        s_new = jnp.exp(b_last)[:, :, 0, :, None] * s + jnp.einsum('bhcd,bhce->bhde', kk * jnp.exp(b_last - b), vv)
        if not with_out:
            return s_new, None
        inter = jnp.einsum('bhcd,bhde->bhce', qq * jnp.exp(b), s)
        decay = jnp.exp(jnp.where(mask, b[:, :, :, None, :] - b[:, :, None, :, :], -jnp.inf))
        attn = jnp.einsum('bhid,bhjd,bhijd->bhij', qq, kk, decay)
        intra = jnp.einsum('bhij,bhje->bhie', attn, vv)
        return s_new, inter + intra

    s_fin, out = lax.scan(step, s0, (to_chunks(q), to_chunks(k), to_chunks(v), to_chunks(log_a)))
    if with_out:
        out = out.transpose(1, 0, 3, 2, 4).reshape(B, L, H, v.shape[-1])
    return s_fin, out

def gla_inputs(zz, af_w2, af_b, ab_w2, ab_b):
    B, L, _ = zz['gla_v'].shape
    f32 = jnp.float32
    q = zz['gla_q'].astype(f32).reshape(B, L, GLA_HEADS, GLA_DK) * GLA_DK ** -0.5
    k = zz['gla_k'].astype(f32).reshape(B, L, GLA_HEADS, GLA_DK)
    v = zz['gla_v'].astype(f32).reshape(B, L, GLA_HEADS, GLA_DV)
    log_a_f = (jax.nn.log_sigmoid((zz['gla_af'] @ af_w2 + af_b).astype(f32)) / GLA_TAU).reshape(B, L, GLA_HEADS, GLA_DK)
    log_a_b = (jax.nn.log_sigmoid((zz['gla_ab'] @ ab_w2 + ab_b).astype(f32)) / GLA_TAU).reshape(B, L, GLA_HEADS, GLA_DK)
    return q, k, v, log_a_f, log_a_b

def gla_output(o, zz, g):
    B, L = o.shape[:2]
    o = rmsnorm(o, g).reshape(B, L, GLA_WIDTH).astype(zz['gla_gate'].dtype)
    return o * jax.nn.silu(zz['gla_gate'])

def gla_branch(z, zc, af_w2, af_b, ab_w2, ab_b, gla_norm, with_ctx_out):
    qc, kc, vc, afc, abc = gla_inputs(zc, af_w2, af_b, ab_w2, ab_b)
    s0 = jnp.zeros((qc.shape[0], GLA_HEADS, GLA_DK, GLA_DV), jnp.float32)
    sc_f, oc_f = gla_scan(qc, kc, vc, afc, s0, with_ctx_out)
    sc_b, oc_b = gla_scan(flip(qc), flip(kc), flip(vc), flip(abc), s0, with_ctx_out)
    q, k, v, af, ab = gla_inputs(z, af_w2, af_b, ab_w2, ab_b)
    _, o_f = gla_scan(q, k, v, af, sc_f, True)
    _, o_b = gla_scan(flip(q), flip(k), flip(v), flip(ab), sc_b, True)
    y = gla_output(o_f + flip(o_b), z, gla_norm)
    yc = gla_output(oc_f + flip(oc_b), zc, gla_norm) if with_ctx_out else None
    return y, yc

def merge_branches(zz, y_mla, y_pool, y_gla, w_bm, w_bp, w_bg, w_out):
    gates = jax.nn.sigmoid(zz['merge'].astype(jnp.float32)).astype(y_mla.dtype)
    g_mla, g_pool, g_gla = jnp.split(gates, N_BRANCH, axis=-1)
    merged = g_mla * (y_mla @ w_bm) + g_pool * (y_pool @ w_bp) + g_gla * (y_gla @ w_bg)
    return merged @ w_out

def trunk_layer(x, xc, mod, mod_c, cos, sin, pre_g, post_g, w_in, mla_q_norm, mla_w_uq, mla_kv_norm,
                mla_w_ukv, pool_w, pool_scale, gla_af_w2, gla_af_b, gla_ab_w2, gla_ab_b, gla_norm,
                w_branch_mla, w_branch_pool, w_branch_gla, w_out, with_ctx_out):
    shift, scale, gate = jnp.split(mod[:, None, :], 3, axis=-1)
    shift_c, scale_c, gate_c = jnp.split(mod_c[None, None, :], 3, axis=-1)
    z = split_columns((rmsnorm(x, pre_g) * (1 + scale) + shift) @ w_in)
    zc = split_columns((rmsnorm(xc, pre_g) * (1 + scale_c) + shift_c) @ w_in)
    y_mla, yc_mla = mla_branch(z, zc, cos, sin, mla_q_norm, mla_w_uq, mla_kv_norm, mla_w_ukv, with_ctx_out)
    y_pool = pool_branch(z, pool_w, pool_scale)
    y_gla, yc_gla = gla_branch(z, zc, gla_af_w2, gla_af_b, gla_ab_w2, gla_ab_b, gla_norm, with_ctx_out)
    out = merge_branches(z, y_mla, y_pool, y_gla, w_branch_mla, w_branch_pool, w_branch_gla, w_out)
    x = x + gate * rmsnorm(out, post_g)
    if with_ctx_out:
        yc_pool = pool_branch(zc, pool_w, pool_scale)
        out_c = merge_branches(zc, yc_mla, yc_pool, yc_gla, w_branch_mla, w_branch_pool, w_branch_gla, w_out)
        xc = xc + gate_c * rmsnorm(out_c, post_g)
    return x, xc

def first_inputs(seed: int = 0) -> dict:
    key = jax.random.key(seed)
    ks = jax.random.split(key, 24)
    f32 = jnp.float32

    def nrm(k, shape, s):
        return jax.random.normal(k, shape, f32) * s

    def gain(k, n):
        return 1.0 + 0.1 * jax.random.normal(k, (DEPTH, n), f32)

    return {
        'x': nrm(ks[0], (BATCH, SEQ, D_MODEL), 1.0),
        'c': nrm(ks[1], (BATCH, D_MODEL), 1.0),
        'ctx': nrm(ks[2], (BATCH, CTX_LEN, D_MODEL), 1.0),
        'c_ctx': nrm(ks[3], (D_MODEL,), 1.0),
        'mod_w': nrm(ks[4], (DEPTH, D_MODEL, 3 * D_MODEL), 0.5 * D_MODEL ** -0.5),
        'mod_b': nrm(ks[5], (DEPTH, 3 * D_MODEL), 0.02),
        'pre_norm': gain(ks[6], D_MODEL),
        'post_norm': gain(ks[7], D_MODEL),
        'w_in': nrm(ks[8], (DEPTH, D_MODEL, D_IN), D_MODEL ** -0.5),
        'mla_q_norm': gain(ks[9], MLA_Q_RANK),
        'mla_w_uq': nrm(ks[10], (DEPTH, MLA_Q_RANK, MLA_HEADS * (MLA_NOPE + MLA_ROPE)), MLA_Q_RANK ** -0.5),
        'mla_kv_norm': gain(ks[11], MLA_KV_RANK),
        'mla_w_ukv': nrm(ks[12], (DEPTH, MLA_KV_RANK, MLA_HEADS * (MLA_NOPE + MLA_V)), MLA_KV_RANK ** -0.5),
        'pool_w': nrm(ks[13], (DEPTH, len(POOL_WINDOWS), POOL_GROUP, POOL_GROUP), POOL_GROUP ** -0.5),
        'pool_scale': gain(ks[14], POOL_WIDTH),
        'gla_af_w2': nrm(ks[15], (DEPTH, GLA_GATE_RANK, GLA_KW), GLA_GATE_RANK ** -0.5),
        'gla_af_b': nrm(ks[16], (DEPTH, GLA_KW), 0.1),
        'gla_ab_w2': nrm(ks[17], (DEPTH, GLA_GATE_RANK, GLA_KW), GLA_GATE_RANK ** -0.5),
        'gla_ab_b': nrm(ks[18], (DEPTH, GLA_KW), 0.1),
        'gla_norm': gain(ks[19], GLA_DV),
        'w_branch_mla': nrm(ks[20], (DEPTH, MLA_WIDTH, D_MODEL), MLA_WIDTH ** -0.5),
        'w_branch_pool': nrm(ks[21], (DEPTH, POOL_WIDTH, D_MODEL), POOL_WIDTH ** -0.5),
        'w_branch_gla': nrm(ks[22], (DEPTH, GLA_WIDTH, D_MODEL), GLA_WIDTH ** -0.5),
        'w_out': nrm(ks[23], (DEPTH, D_MODEL, D_MODEL), D_MODEL ** -0.5),
    }

def first_block(x, c, ctx, c_ctx, mod_w, mod_b, pre_norm, post_norm, w_in, mla_q_norm, mla_w_uq,
              mla_kv_norm, mla_w_ukv, pool_w, pool_scale, gla_af_w2, gla_af_b, gla_ab_w2, gla_ab_b,
              gla_norm, w_branch_mla, w_branch_pool, w_branch_gla, w_out):
    n_tok = x.shape[1]
    rows = n_tok // GRID_W
    row = jnp.repeat(jnp.arange(rows), GRID_W)
    col = jnp.tile(jnp.arange(GRID_W), rows)
    cos, sin = axial_rope_tables(row, col)
    silu_c = jax.nn.silu(c)
    silu_cc = jax.nn.silu(c_ctx)
    xc = ctx
    for l in range(DEPTH):
        mod = silu_c @ mod_w[l] + mod_b[l]
        mod_c = silu_cc @ mod_w[l] + mod_b[l]
        x, xc = trunk_layer(x, xc, mod, mod_c, cos, sin, pre_norm[l], post_norm[l], w_in[l],
                            mla_q_norm[l], mla_w_uq[l], mla_kv_norm[l], mla_w_ukv[l], pool_w[l],
                            pool_scale[l], gla_af_w2[l], gla_af_b[l], gla_ab_w2[l], gla_ab_b[l],
                            gla_norm[l], w_branch_mla[l], w_branch_pool[l], w_branch_gla[l], w_out[l],
                            l < DEPTH - 1)
    return x


CHUNK = 64
N_LEFT_CHUNKS = 8
BAND = (N_LEFT_CHUNKS + 1) * CHUNK
HEAD_DIM = 64
N_HEADS_A = 8
N_HEADS_B = 8
A_W = N_HEADS_A * HEAD_DIM
B_W = N_HEADS_B * HEAD_DIM
MIX_W = A_W + B_W
REL_CLIP = 256
LRU_WIDTH = D_MODEL
LRU_BLOCKS = 4
LRU_BLOCK_W = LRU_WIDTH // LRU_BLOCKS
CONV_WIDTH = 4
LRU_C = 8.0
D_FF = -(-(8 * D_MODEL) // (3 * 256)) * 256
RMS_EPS = 1e-6
N_ATTN_LAYERS = (DEPTH + 1) // 2
N_REC_LAYERS = DEPTH // 2


def rmsnorm_2(x, g):
    xf = x.astype(jnp.float32)
    y = xf * lax.rsqrt(jnp.mean(xf * xf, axis=-1, keepdims=True) + RMS_EPS)
    return (y * g.astype(jnp.float32)).astype(x.dtype)

def chunked_relpos_attention(q, k, v, rel_bias):
    b, s, h, dh = q.shape
    nc = s // CHUNK
    qc = q.reshape(b, nc, CHUNK, h, dh)

    def gather_band(t):
        tc = t.reshape(b, nc, CHUNK, h, dh)
        tp = jnp.pad(tc, ((0, 0), (N_LEFT_CHUNKS, 0), (0, 0), (0, 0), (0, 0)))
        return jnp.concatenate([tp[:, j:j + nc] for j in range(N_LEFT_CHUNKS + 1)], axis=2)

    kb, vb = gather_band(k), gather_band(v)
    scores = jnp.einsum('bcqhd,bckhd->bhcqk', qc, kb).astype(jnp.float32) * (dh ** -0.5)
    qpos = N_LEFT_CHUNKS * CHUNK + jnp.arange(CHUNK)
    kpos = jnp.arange(BAND)
    rel = jnp.clip(qpos[:, None] - kpos[None, :], -REL_CLIP, REL_CLIP) + REL_CLIP
    bias = rel_bias[:, rel].astype(jnp.float32)
    key_chunk = jnp.arange(nc)[:, None] - N_LEFT_CHUNKS + (kpos // CHUNK)[None, :]
    valid = key_chunk >= 0
    scores = scores + bias[None, :, None, :, :]
    scores = jnp.where(valid[None, None, :, None, :], scores, -jnp.inf)
    p = jax.nn.softmax(scores, axis=-1).astype(v.dtype)
    o = jnp.einsum('bhcqk,bckhd->bcqhd', p, vb)
    return o.reshape(b, s, h * dh)

def stick_breaking_attention(q, k, v):
    b, s, h, dh = q.shape
    nb = s // Q_BLOCK
    scale = dh ** -0.5
    kpos = jnp.arange(s)
    q_blocks = q.reshape(b, nb, Q_BLOCK, h, dh).transpose(1, 0, 2, 3, 4)

    def one_block(args):
        q_blk, blk = args
        z = jnp.einsum('bqhd,bkhd->bhqk', q_blk, k).astype(jnp.float32) * scale
        qpos = blk * Q_BLOCK + jnp.arange(Q_BLOCK)
        causal = kpos[None, :] < qpos[:, None]
        log_beta = jax.nn.log_sigmoid(z)
        log_1m_beta = jnp.where(causal, jax.nn.log_sigmoid(-z), 0.0)
        after = lax.cumsum(log_1m_beta, axis=3, reverse=True) - log_1m_beta
        w = jnp.where(causal, jnp.exp(log_beta + after), 0.0).astype(v.dtype)
        return jnp.einsum('bhqk,bkhd->bqhd', w, v)

    o = lax.map(one_block, (q_blocks, jnp.arange(nb)))
    return o.transpose(1, 0, 2, 3, 4).reshape(b, s, h * dh)

def attention_mixer(h, w_in, rel_bias, w_out):
    b, s, _ = h.shape
    proj = h @ w_in
    part_a, part_b = proj[..., :3 * A_W], proj[..., 3 * A_W:]
    qa, ka, va = [t.reshape(b, s, N_HEADS_A, HEAD_DIM) for t in jnp.split(part_a, 3, axis=-1)]
    qs, ks, vs = [t.reshape(b, s, N_HEADS_B, HEAD_DIM) for t in jnp.split(part_b, 3, axis=-1)]
    out_a = chunked_relpos_attention(qa, ka, va, rel_bias)
    out_b = stick_breaking_attention(qs, ks, vs)
    return jnp.concatenate([out_a, out_b], axis=-1) @ w_out

def recurrent_mixer(h, w_in, conv_w, conv_b, w_a, b_a, w_i, b_i, lam, w_out):
    b, s, _ = h.shape
    proj = h @ w_in
    gate, xr = jnp.split(proj, 2, axis=-1)
    gate = jax.nn.gelu(gate, approximate=True)
    xc = lax.conv_general_dilated(
        xr, conv_w, window_strides=(1,), padding=[(CONV_WIDTH - 1, 0)],
        dimension_numbers=('NWC', 'WIO', 'NWC'), feature_group_count=LRU_WIDTH) + conv_b
    xg = xc.reshape(b, s, LRU_BLOCKS, LRU_BLOCK_W)
    r = jax.nn.sigmoid(jnp.einsum('bsni,nij->bsnj', xg, w_a) + b_a).reshape(b, s, LRU_WIDTH)
    i = jax.nn.sigmoid(jnp.einsum('bsni,nij->bsnj', xg, w_i) + b_i).reshape(b, s, LRU_WIDTH)
    log_a = -LRU_C * r.astype(jnp.float32) * jax.nn.softplus(-lam.astype(jnp.float32))
    a = jnp.exp(log_a)
    mult = jnp.sqrt(-jnp.expm1(2.0 * log_a))
    u = mult * (i * xc).astype(jnp.float32)

    def combine(left, right):
        a1, b1 = left
        a2, b2 = right
        return a1 * a2, a2 * b1 + b2

    _, hs = lax.associative_scan(combine, (a, u), axis=1)
    return (hs.astype(h.dtype) * gate) @ w_out

def swiglu(h, w_gate, w_up, w_down):
    return (jax.nn.silu(h @ w_gate) * (h @ w_up)) @ w_down

def second_inputs(seed: int = 0) -> dict:
    key = jax.random.key(seed)
    ks = jax.random.split(key, 24)
    f32 = jnp.float32

    def nrm(k, shape, fan_in):
        return jax.random.normal(k, shape, f32) * (fan_in ** -0.5)

    def gain(k, shape):
        return 1.0 + 0.05 * jax.random.normal(k, shape, f32)

    u = jax.random.uniform(ks[12], (N_REC_LAYERS, LRU_WIDTH), f32, 0.9, 0.999)
    base = u ** (1.0 / LRU_C)
    lam = jnp.log(base) - jnp.log1p(-base)
    return {
        'x': jax.random.normal(ks[0], (BATCH, SEQ, D_MODEL), f32),
        'attn_w_in': nrm(ks[1], (N_ATTN_LAYERS, D_MODEL, 3 * MIX_W), D_MODEL),
        'attn_rel_bias': 0.2 * jax.random.normal(ks[2], (N_ATTN_LAYERS, N_HEADS_A, 2 * REL_CLIP + 1), f32),
        'attn_w_out': nrm(ks[3], (N_ATTN_LAYERS, MIX_W, D_MODEL), MIX_W),
        'rg_w_in': nrm(ks[4], (N_REC_LAYERS, D_MODEL, 2 * LRU_WIDTH), D_MODEL),
        'rg_conv_w': nrm(ks[5], (N_REC_LAYERS, CONV_WIDTH, 1, LRU_WIDTH), CONV_WIDTH),
        'rg_conv_b': 0.01 * jax.random.normal(ks[6], (N_REC_LAYERS, LRU_WIDTH), f32),
        'rg_w_a': nrm(ks[7], (N_REC_LAYERS, LRU_BLOCKS, LRU_BLOCK_W, LRU_BLOCK_W), LRU_BLOCK_W),
        'rg_b_a': 0.01 * jax.random.normal(ks[8], (N_REC_LAYERS, LRU_BLOCKS, LRU_BLOCK_W), f32),
        'rg_w_i': nrm(ks[9], (N_REC_LAYERS, LRU_BLOCKS, LRU_BLOCK_W, LRU_BLOCK_W), LRU_BLOCK_W),
        'rg_b_i': 0.01 * jax.random.normal(ks[10], (N_REC_LAYERS, LRU_BLOCKS, LRU_BLOCK_W), f32),
        'rg_lambda': lam,
        'rg_w_out': nrm(ks[11], (N_REC_LAYERS, LRU_WIDTH, D_MODEL), LRU_WIDTH),
        'norm_mix_pre': gain(ks[13], (DEPTH, D_MODEL)),
        'norm_mix_post': gain(ks[14], (DEPTH, D_MODEL)),
        'norm_ffn_pre': gain(ks[15], (DEPTH, D_MODEL)),
        'norm_ffn_post': gain(ks[16], (DEPTH, D_MODEL)),
        'ffn_w_gate': nrm(ks[17], (DEPTH, D_MODEL, D_FF), D_MODEL),
        'ffn_w_up': nrm(ks[18], (DEPTH, D_MODEL, D_FF), D_MODEL),
        'ffn_w_down': nrm(ks[19], (DEPTH, D_FF, D_MODEL), D_FF),
    }

def second_block(x, attn_w_in, attn_rel_bias, attn_w_out, rg_w_in, rg_conv_w, rg_conv_b,
              rg_w_a, rg_b_a, rg_w_i, rg_b_i, rg_lambda, rg_w_out,
              norm_mix_pre, norm_mix_post, norm_ffn_pre, norm_ffn_post,
              ffn_w_gate, ffn_w_up, ffn_w_down):
    for layer in range(DEPTH):
        j = layer // 2
        h = rmsnorm_2(x, norm_mix_pre[layer])
        if layer % 2 == 0:
            m = attention_mixer(h, attn_w_in[j], attn_rel_bias[j], attn_w_out[j])
        else:
            m = recurrent_mixer(h, rg_w_in[j], rg_conv_w[j], rg_conv_b[j], rg_w_a[j], rg_b_a[j],
                                rg_w_i[j], rg_b_i[j], rg_lambda[j], rg_w_out[j])
        x = x + rmsnorm_2(m, norm_mix_post[layer])
        h = rmsnorm_2(x, norm_ffn_pre[layer])
        f = swiglu(h, ffn_w_gate[layer], ffn_w_up[layer], ffn_w_down[layer])
        x = x + rmsnorm_2(f, norm_ffn_post[layer])
    return x


def setup_inputs(seed=0):
    out = dict(first_inputs(seed))
    for name, value in second_inputs(seed + 1).items():
        if name != "x":
            out[name + "_2"] = value
    return out


def reference(
    x, c, ctx, c_ctx, mod_w, mod_b, pre_norm, post_norm, w_in, mla_q_norm, mla_w_uq,
    mla_kv_norm, mla_w_ukv, pool_w, pool_scale, gla_af_w2, gla_af_b, gla_ab_w2, gla_ab_b,
    gla_norm, w_branch_mla, w_branch_pool, w_branch_gla, w_out, attn_w_in_2, attn_rel_bias_2,
    attn_w_out_2, rg_w_in_2, rg_conv_w_2, rg_conv_b_2, rg_w_a_2, rg_b_a_2, rg_w_i_2, rg_b_i_2,
    rg_lambda_2, rg_w_out_2, norm_mix_pre_2, norm_mix_post_2, norm_ffn_pre_2, norm_ffn_post_2,
    ffn_w_gate_2, ffn_w_up_2, ffn_w_down_2,
):
    x = first_block(
        x, c, ctx, c_ctx, mod_w, mod_b, pre_norm, post_norm, w_in, mla_q_norm, mla_w_uq,
        mla_kv_norm, mla_w_ukv, pool_w, pool_scale, gla_af_w2, gla_af_b, gla_ab_w2, gla_ab_b,
        gla_norm, w_branch_mla, w_branch_pool, w_branch_gla, w_out,
    )
    return second_block(
        x, attn_w_in_2, attn_rel_bias_2, attn_w_out_2, rg_w_in_2, rg_conv_w_2, rg_conv_b_2,
        rg_w_a_2, rg_b_a_2, rg_w_i_2, rg_b_i_2, rg_lambda_2, rg_w_out_2, norm_mix_pre_2,
        norm_mix_post_2, norm_ffn_pre_2, norm_ffn_post_2, ffn_w_gate_2, ffn_w_up_2,
        ffn_w_down_2,
    )


_drawn_inputs = setup_inputs


def setup_inputs(seed=0):
    import zlib

    import numpy as np

    out = dict(_drawn_inputs(seed))
    spreads = {}
    factors = {'mla_q_norm': 8.0,
     'mla_kv_norm': 3.703,
     'gla_af_b': 3.636,
     'gla_ab_b': 3.651,
     'rg_b_a_2': 54.526,
     'rg_b_i_2': 27.386}
    for name, (base, spread) in spreads.items():
        noise = np.random.default_rng([zlib.crc32(name.encode()), seed]).standard_normal(out[name].shape)
        drawn = base * np.exp(spread * noise) if base else spread * noise
        out[name] = jnp.asarray(drawn.astype(out[name].dtype))
    for name, factor in factors.items():
        out[name] = (out[name] * factor).astype(out[name].dtype)
    return out
```

```python
import concourse.bass as bass
from concourse import mybir
from contextlib import ExitStack

P = 128
D = 1024
KT = D // P
SEQ, CTX = 256, 256
TOK = CTX + SEQ
DEPTH = 2
QR, KVR = 256, 128
HEADS, NOPE, ROPE, VD = 8, 64, 32, 64
QKD = NOPE + ROPE
GH, GDK, GDV, GCH = 4, 64, 128, 128
NCH = TOK // GCH
WINDOWS = (2, 4, 8, 16)
PADW = max(WINDOWS) // 2
DFF = 2816
FB = DFF // P
NORM_EPS = 1e-6
CLAMP = 80.0

SLOTS = 4
PANEL = 16 * P
PLAN = {}


def plan():
    at = 0
    for l in range(DEPTH):
        for name, n in (("mod", 12), ("win", 12), ("gv", 2), ("merge", 18), ("wout", 4)):
            PLAN[name, l] = at
            at += n
    for name, n in (("attn_qk", 8), ("attn_v", 4), ("attn_out", 4), ("gate_up0", 22), ("down0", 11),
                    ("rg_in", 8), ("rg_ai", 2), ("rg_out", 4), ("gate_up1", 22), ("down1", 11)):
        PLAN[name] = at
        at += n
    return at


PANELS = plan()

Z_KV, Z_MISC, Z_GK, Z_GQ, Z_QLAT, Z_POOL, Z_GATE = 0, 1, 2, 4, 6, 8, 12
AF, AB, KR = 0, 32, 64

VEC = {}


def vectors():
    at = 0
    for name, n in (("c", 2 * KT), ("mod_b", DEPTH * 2 * 3 * KT), ("pre", DEPTH * KT), ("post", DEPTH * KT),
                    ("qn", DEPTH * 2), ("kvn", DEPTH), ("pscale", DEPTH * 4), ("gab", DEPTH * 4), ("gn", DEPTH),
                    ("mixpre", DEPTH * KT), ("mixpost", DEPTH * KT), ("ffnpre", DEPTH * KT),
                    ("ffnpost", DEPTH * KT), ("convw", 4 * KT), ("convb", KT), ("ba", KT), ("bi", KT), ("lam", KT), ("eps", 1)):
        VEC[name] = at
        at += n
    return at


NVEC = vectors()
SW_UQ, SW_UK, SW_UV, SW_PW, SW_DW = 0, 1536, 2048, 2560, 3072
NSW = 3328
C_ONES, C_ID, C_MASK, C_COS, C_SIN, C_ROT, C_EDGE = 0, 256, 384, 640, 896, 1152, 1184
NCONST = C_EDGE + 4 * 2 * PADW


order = ([0, 1, 2, 3], [1, 0, 3, 2])


def mla_units(l):
    return [(h, qb, CTX if qb < 2 else TOK) for h in range(HEADS) for qb in range(0 if l == 0 else 2, 4)]


b2_units = [(h, qb, SEQ) for h in range(HEADS) for qb in range(2)]


def program(nc, x_t, wstream, small, vecs, consts, rel, consts2, out_t):
    f32 = mybir.dt.float32
    ALU = mybir.AluOpType
    ACT = mybir.ActivationFunctionType
    AX = mybir.AxisListType.X
    CT, XT, AT_ = slice(0, CTX), slice(CTX, TOK), slice(0, TOK)

    with ExitStack() as ctx:
        def sb(name, *shape):
            return ctx.enter_context(nc.sbuf_tensor(name, [P, *shape], f32))

        def sem(name):
            return ctx.enter_context(nc.semaphore(name))

        ring = sb("ring", SLOTS, PANEL)
        X = sb("X", KT, TOK)
        XN = sb("XN", KT, TOK)
        Z = sb("Z", 24, TOK)
        VG = sb("VG", 4, 512)
        VM = sb("VM", 4, 512)
        SQ = sb("SQ", KT, TOK)
        QB = sb("QB", KT, TOK)
        KB = sb("KB", KT, TOK)
        PR = sb("PR", 2, 512)
        PT = sb("PT", 4, P)
        RA = sb("RA", 512)
        SW = sb("SW", NSW)
        V = sb("V", NVEC)
        C = sb("C", NCONST)
        MOD = sb("MOD", 3 * KT, 2)
        AMOD = sb("AMOD", KT, 2)
        GPOST = sb("GPOST", KT, 2)
        NLAM = sb("NLAM", KT)
        LT = sb("LT", 4, KT)
        STAT = sb("STAT", 2, 4)
        G = [ctx.enter_context(nc.psum_tensor(f"G{i}", [P, 512], f32)) for i in range(4)]
        S = [ctx.enter_context(nc.psum_tensor(f"S{i}", [P, 512], f32)) for i in range(2)]
        DB = [ctx.enter_context(nc.psum_tensor(f"D{i}", [P, 512], f32)) for i in range(2)]

        def flat(t):
            return t[:, :, :].rearrange("p a b -> p (a b)")

        KDT = VM[:, :, :].rearrange("p a (b c) -> p (a b) c", c=P)
        LG = Z[:, Z_POOL:Z_POOL + 4, :]
        EX = SQ[:, 0:4, :]
        EE = SQ[:, 4:8, :]
        QTB, QEB = QB[:, 0:4, :], QB[:, 4:8, :]
        KTB, KDB = KB[:, 0:4, :], KB[:, 4:8, :]
        ST = [PR[:, 0, :], PR[:, 1, :], flat(PT)]
        OG = Z[:, Z_GK:Z_GK + 4, :]
        CS = flat(SQ)[:, 0:4 * (SEQ + 2 * PADW)].rearrange("p (g t) -> p g t", g=4)
        PB = SQ[:, 4:8, :]
        MROW = flat(KB)[:, 0:3 * D]
        ones = C[:, C_ONES:C_ONES + 256]
        ident = C[:, C_ID:C_ID + P]
        H = flat(Z)[:, 0:FB * SEQ].rearrange("p (f t) -> p f t", f=FB)
        BT = Z[:, 16:24, :].rearrange("p a (b t) -> p (a b) t", t=SEQ)
        YB = KB[:, :, 0:SEQ]
        strict, strict_neg, causal_neg = X[:, 0:2, CT], X[:, 2:4, CT], X[:, 4:6, CT]

        def gatt(i):
            return Z[:, Z_QLAT + i % 2, :].rearrange("p (a b) -> p a b", b=P)

        def vec(name, i):
            return V[:, VEC[name] + i:VEC[name] + i + 1]

        def seg(t):
            return 1 if t is XT else 0

        panel_in = [sem(f"panel_in{i}") for i in range(SLOTS)]
        const_in, x_in, small_in, bias_in, out_done = sem("const_in"), sem("x_in"), sem("small_in"), sem("bias_in"), sem("out_done")
        halves_done = sem("halves_done")
        g_ready, g_free = sem("g_ready"), sem("g_free")
        s_ready, s_free = sem("s_ready"), sem("s_free")
        d_ready, d_free = sem("d_ready"), sem("d_free")
        dve_step, act_step = sem("dve_step"), sem("act_step")
        silu_c_ready, modrow_ready = sem("silu_c_ready"), sem("modrow_ready")
        sq_ready, rstd_ready, xn_ready = sem("sq_ready"), sem("rstd_ready"), sem("xn_ready")
        block_ready = sem("block_ready")
        z_ready, gates_ready = sem("z_ready"), sem("gates_ready")
        gv_ready, lat_ready, qkv_ready = sem("gv_ready"), sem("lat_ready"), sem("qkv_ready")
        qcopy_ready = sem("qcopy_ready")
        kr_ready, kr_copied = sem("kr_ready"), sem("kr_copied")
        turned, rowmax_ready, prob_ready, probn_ready, pt_ready, pv_done = (
            sem("turned"), sem("rowmax_ready"), sem("prob_ready"), sem("probn_ready"), sem("pt_ready"), sem("pv_done"))
        pooled_ready = sem("pooled_ready")
        logit_ready, soft_ready, expo_ready, exp_ready, decayed = (
            sem("logit_ready"), sem("soft_ready"), sem("expo_ready"), sem("exp_ready"), sem("decayed"))
        kdt_ready, state_ready, gatt_ready, og_ready = (
            sem("kdt_ready"), sem("state_ready"), sem("gatt_ready"), sem("og_ready"))
        gla_done = sem("gla_done")
        merged_ready, block1_free = sem("merged_ready"), sem("block1_free")
        silu_ready, log_a_ready = sem("silu_ready"), sem("log_a_ready")
        layer_done = sem("layer_done")

        block = ctx.enter_context(nc.Block())

        class Count:

            def __init__(self):
                self.n = {}

            def next(self, s, k=1):
                self.n[s.name] = self.n.get(s.name, 0) + k
                return self.n[s.name]

            def at(self, s):
                return self.n.get(s.name, 0)

        @block.sync
        def _(sp):
            sp.dma_start(V[:, :], vecs).then_inc(const_in, 16)
            sp.dma_start(X[:, :, :], x_t).then_inc(x_in, 16)
            sp.dma_start(C[:, :], consts).then_inc(const_in, 16)
            for s in range(SLOTS):
                sp.dma_start(ring[:, s, :], wstream[s]).then_inc(panel_in[s], 16)
            with sp.Fori(0, PANELS // SLOTS - 1) as g:
                for s in range(SLOTS):
                    sp.wait_ge(halves_done, g * (2 * SLOTS) + 2 * (s + 1))
                    sp.dma_start(ring[:, s, :], wstream[bass.ds(g * SLOTS + (s + SLOTS), 1), :, :]
                                 .rearrange("a p c -> (a p) c")).then_inc(panel_in[s], 16)
            sp.wait_ge(layer_done, 6)
            sp.dma_start(out_t, X[:, :, XT]).then_inc(out_done, 16)
            sp.wait_ge(out_done, 16)

        @block.gpsimd
        def _(pool):
            pool.dma_start(SW[:, :], small[0]).then_inc(small_in, 16)
            pool.wait_ge(gla_done, 1)
            pool.dma_start(SW[:, :], small[1]).then_inc(small_in, 16)
            pool.wait_ge(block1_free, 1)
            pool.dma_start(BT, rel).then_inc(bias_in, 16)
            pool.dma_start(X[:, 0:6, CT], consts2).then_inc(bias_in, 16)

        @block.tensor
        def _(pe):
            n = Count()
            blocks = Count()

            def panel_wait(p):
                pe.wait_ge(panel_in[p % SLOTS], 16 * (p // SLOTS + 1))

            def tile(p, t, m=P):
                return ring[:, p % SLOTS, t * P:t * P + m]

            def g_bank(base=None, i=0):
                if base is not None:
                    pe.wait_ge(g_free, base + i - 3)
                    return G[(blocks.at(g_free) + i) % 4]
                b = blocks.next(g_free) - 1
                if b >= 4:
                    pe.wait_ge(g_free, b - 3)
                return G[b % 4]

            def d_bank():
                b = n.next(d_ready) - 1
                if b >= 2:
                    pe.wait_ge(d_free, b - 1)
                return DB[b % 2]

            def s_bank():
                b = n.next(s_ready) - 1
                if b >= 2:
                    pe.wait_ge(s_free, b - 1)
                return S[b % 2]

            def product(out, pairs):
                for i, (w, x) in enumerate(pairs):
                    last = nc.tensor.matmul(out, w, x, start=i == 0, stop=i == len(pairs) - 1)
                return last

            def columns(p, src, t, per_half=1, kts=KT):
                panel_wait(p)
                for half in range(2):
                    for b in range(per_half):
                        bank = g_bank()
                        last = product(bank[:, 0:t.stop - t.start],
                                       [(tile(p, (half * per_half + b) * kts + k), src[:, k, t]) for k in range(kts)])
                    last.then_inc(halves_done, 1)

            def columns_loop(p0, panels, src, t):
                base = blocks.at(g_free)
                with pe.Fori(0, panels // SLOTS) as g:
                    for u in range(SLOTS):
                        s = (p0 + u) % SLOTS
                        pe.wait_ge(panel_in[s], g * 16 + 16 * ((p0 + u) // SLOTS + 1))
                        for half in range(2):
                            i = 2 * u + half
                            pe.wait_ge(g_free, g * (2 * SLOTS) + (base + i - 3))
                            product(G[(base + i) % 4][:, 0:t.stop - t.start],
                                    [(tile(s, half * KT + k), src[:, k, t]) for k in range(KT)]
                                    ).then_inc(halves_done, 1)
                blocks.next(g_free, 2 * panels)

            def token_rows(p, src, tbs):
                panel_wait(p)
                for i, tb in enumerate(tbs):
                    bank = g_bank()
                    last = product(bank[:, 0:256], [(src[:, k, tb * P:(tb + 1) * P], ring[:, p % SLOTS, k * 256:(k + 1) * 256])
                                                    for k in range(KT)])
                    if i < len(tbs) - 1:
                        last.then_inc(g_ready, 1)
                last.then_inc(halves_done, 2)

            def norm_sum(parts, t):
                for part in parts:
                    bank = s_bank()
                    for i, k in enumerate(part):
                        if k % 2 == 0 or i == 0:
                            pe.wait_ge(sq_ready, n.next(sq_ready))
                        last = nc.tensor.matmul(bank[:, 0:t.stop - t.start], ones[:, 0:P], SQ[:, k, t],
                                                start=i == 0, stop=i == len(part) - 1)
                    last.then_inc(s_ready, 1)

            def transposes(src, count):
                bank = d_bank()
                for i in range(count):
                    last = nc.tensor.transpose(bank[:, i * P:(i + 1) * P], src[:, i * P:(i + 1) * P], ident)
                last.then_inc(d_ready, 1)

            def attention(units, score, values, pt):
                first_qb, last = units[0][1], len(units) - 1
                pe.wait_ge(d_free, n.at(d_ready))
                state = {}

                def turn(i):
                    pe.wait_ge(probn_ready, n.next(probn_ready))
                    for k in range(units[i][2] // P):
                        last_t = nc.tensor.transpose(DB[i % 2][:, k * P:(k + 1) * P], PR[:, i % 2, k * P:(k + 1) * P], ident)
                    last_t.then_inc(turned, 1)

                def weigh(i):
                    h, qb, nk = units[i]
                    if h % 2 == 0 and qb == first_qb:
                        state["bank"] = g_bank()
                    pe.wait_ge(pt_ready, n.next(pt_ready))
                    cols = slice((qb - first_qb) * P, (qb - first_qb + 1) * P)
                    b = VD * (h % 2)
                    product(state["bank"][b:b + VD, cols], [(values(k, h), pt[:, i % 2, k * P:(k + 1) * P]) for k in range(nk // P)]
                            ).then_inc(pv_done, 1)

                for i in range(-2, len(units)):
                    if i + 2 <= last:
                        score(s_bank(), *units[i + 2]).then_inc(s_ready, 1)
                    if 0 <= i + 1 <= last:
                        turn(i + 1)
                    if i >= 0:
                        weigh(i)

            def mod(l):
                p0 = PLAN["mod", l]
                if l == 0:
                    pe.wait_ge(silu_c_ready, 1)
                for c in range(6):
                    bank = g_bank()
                    for i in range(2):
                        p = p0 + 2 * c + i
                        panel_wait(p)
                        for k in range(4):
                            at = VEC["c"] + 2 * (4 * i + k)
                            last = nc.tensor.matmul(bank[0:2, :], V[:, at:at + 2], ring[:, p % SLOTS, k * 512:(k + 1) * 512],
                                                    start=i == 0 and k == 0, stop=i == 1 and k == 3)
                        last.then_inc(halves_done, 2)
                bank = g_bank()
                pe.wait_ge(modrow_ready, l + 1)
                for m in range(3 * KT):
                    last = nc.tensor.transpose(bank[:, 2 * m:2 * m + 2], MROW[0:2, m * P:(m + 1) * P], ident[0:2, 0:2])
                last.then_inc(g_ready, 1)

            def first_block(l):
                t = AT_ if l == 0 else XT
                mod(l)
                norm_sum([range(KT)], AT_)
                pe.wait_ge(xn_ready, n.next(xn_ready))
                p0 = PLAN["win", l]
                for u in range(4):
                    columns(p0 + u, XN, AT_)
                columns_loop(p0 + 4, 8, XN, t)
                for i in range(2):
                    token_rows(PLAN["gv", l] + i, XN, range(4))

                norm_sum([[0], [2, 3]], AT_)
                pe.wait_ge(lat_ready, n.next(lat_ready))
                pe.wait_ge(small_in, 16 * (l + 1))
                for h in range(HEADS):
                    product(d_bank()[0:QKD, 0:t.stop - t.start],
                            [(SW[:, SW_UQ + k * 768 + h * QKD:SW_UQ + k * 768 + (h + 1) * QKD], Z[:, Z_QLAT + k, t])
                             for k in range(2)]).then_inc(d_ready, 1)
                for h in range(HEADS):
                    product(d_bank()[0:NOPE, :], [(SW[:, SW_UK + h * NOPE:SW_UK + (h + 1) * NOPE], Z[:, Z_KV, :])]
                            ).then_inc(d_ready, 1)
                for tb in range(4):
                    product(d_bank()[:, :], [(Z[:, Z_KV, tb * P:(tb + 1) * P], SW[:, SW_UV:SW_UV + 512])]
                            ).then_inc(d_ready, 1)
                rot = C[KR:KR + ROPE, C_ROT:C_ROT + ROPE]
                product(d_bank()[KR:KR + ROPE, 0:SEQ], [(rot, Z[KR:KR + ROPE, Z_MISC, XT])]).then_inc(d_ready, 1)
                pe.wait_ge(qcopy_ready, n.next(qcopy_ready))
                for h in range(0, HEADS, 2):
                    product(d_bank()[KR:KR + ROPE, :].rearrange("p (h t) -> p h t", h=2),
                            [(rot, QB[KR:KR + ROPE, h:h + 2, XT])]).then_inc(d_ready, 1)
                pe.wait_ge(qkv_ready, n.next(qkv_ready))
                pe.wait_ge(kr_copied, n.next(kr_copied))
                attention(mla_units(l),
                          lambda bank, h, qb, nk: product(bank[:, 0:nk], [(QB[0:QKD, h, qb * P:(qb + 1) * P], KB[0:QKD, h, 0:nk])]),
                          lambda k, h: VM[:, k, h * VD:(h + 1) * VD], Z[:, Z_QLAT:Z_QLAT + 2, :])
                pe.wait_ge(pooled_ready, n.next(pooled_ready))
                for g in range(4):
                    product(d_bank()[:, 0:t.stop - t.start], [(SW[:, SW_PW + g * P:SW_PW + (g + 1) * P], PB[:, g, t])]
                            ).then_inc(d_ready, 1)
                for d, row in ((0, AF), (1, AB)):
                    for j in range(2):
                        product(d_bank()[:, :], [(SW[row:row + 16, SW_DW + j * P:SW_DW + (j + 1) * P], Z[row:row + 16, Z_MISC, :])]
                                ).then_inc(d_ready, 1)
                for d in range(2):
                    pe.wait_ge(decayed, n.next(decayed))
                    for j in range(2):
                        transposes(KDB[:, 2 * d + j, :], NCH)
                pe.wait_ge(kdt_ready, n.next(kdt_ready))
                for step in range(3):
                    bank = d_bank()
                    for d in range(2):
                        c = order[d][step]
                        for j in range(2):
                            for e in range(2):
                                h = 2 * j + e
                                col = (2 * d + j) * P
                                last = nc.tensor.matmul(bank[e * GDK:(e + 1) * GDK, col:col + GDV],
                                                        KDT[:, (2 * d + j) * NCH + c, e * GDK:(e + 1) * GDK],
                                                        VG[:, c, h * GDV:(h + 1) * GDV], start=True, stop=True)
                    last.then_inc(d_ready, 1)
                pe.wait_ge(state_ready, n.next(state_ready))
                first = 0 if l == 0 else 2
                for j in range(2):
                    banks = [g_bank(), g_bank()]
                    for c in range(first, NCH):
                        cc = slice(c * GCH, (c + 1) * GCH)
                        for e in range(2):
                            r = slice(e * GDK, (e + 1) * GDK)
                            bank = d_bank()
                            for d in range(2):
                                last = nc.tensor.matmul(bank[:, d * P:(d + 1) * P], KTB[r, 2 * d + j, cc],
                                                        QTB[r, 2 * d + j, cc], start=True, stop=True)
                            last.then_inc(d_ready, 1)
                        pe.wait_ge(gatt_ready, n.next(gatt_ready, 2))
                        for e in range(2):
                            r = slice(e * GDK, (e + 1) * GDK)
                            h = 2 * j + e
                            pairs = [(VG[:, c, h * GDV:(h + 1) * GDV], gatt(n.at(gatt_ready) // 2)[:, 2 * e + d, :]) for d in range(2)]
                            for d in range(2):
                                step = order[d].index(c) - 1
                                if step >= 0:
                                    pairs.append((ST[step][r, (2 * d + j) * P:(2 * d + j + 1) * P], QEB[r, 2 * d + j, cc]))
                            last = product(banks[e][:, (c - first) * GCH:(c - first + 1) * GCH], pairs)
                        last.then_inc(g_ready, 1)
                norm_sum([[0], [1], [2], [3]], t)
                pe.wait_ge(gla_done, n.next(gla_done))
                p0 = PLAN["merge", l]
                for b in range(3):
                    for u in range(4):
                        columns(p0 + 6 * b + u, XN, t)
                    for u in range(2):
                        columns(p0 + 6 * b + 4 + u, Z[:, Z_GATE + 4 * b:Z_GATE + 4 * b + 4, :], t, per_half=2, kts=4)
                pe.wait_ge(merged_ready, n.next(merged_ready, 3))
                columns_loop(PLAN["wout", l], 4, KB, t)
                norm_sum([range(KT)], t)

            def pre_norm():
                norm_sum([range(KT)], XT)
                pe.wait_ge(xn_ready, n.next(xn_ready))

            def ffn(i):
                pre_norm()
                p0 = PLAN[f"gate_up{i}"]
                columns_loop(p0, 20, XN, XT)
                columns(p0 + 20, XN, XT)
                columns(p0 + 21, XN, XT)
                pe.wait_ge(g_free, blocks.at(g_free))
                pe.wait_ge(s_free, n.at(s_ready))
                pe.wait_ge(d_free, n.at(d_ready))
                banks = [g_bank() for _ in range(4)] + [*S, *DB]
                for u in range(11):
                    p = PLAN[f"down{i}"] + u
                    panel_wait(p)
                    for k in range(2):
                        for m in range(KT):
                            last = nc.tensor.matmul(banks[m][:, 0:SEQ], tile(p, k * KT + m), H[:, 2 * u + k, :],
                                                    start=u == 0 and k == 0, stop=u == 10 and k == 1)
                        last.then_inc(halves_done, 1)
                pe.wait_ge(block_ready, n.next(block_ready))
                norm_sum([range(KT)], XT)

            pe.wait_ge(const_in, 32)
            for l in range(DEPTH):
                first_block(l)
            pre_norm()
            columns_loop(PLAN["attn_qk"], 8, XN, XT)
            for i in range(4):
                token_rows(PLAN["attn_v"] + i, XN, (2, 3))
            for kind, base, values in (("rel", 0, VG), ("stick", 8, VM)):
                pe.wait_ge(z_ready, n.next(z_ready))

                def score(bank, h, qb, nk, base=base):
                    r = slice(64 * (h % 2), 64 * (h % 2) + 64)
                    return product(bank[:, 0:nk], [(Z[r, base + h // 2, CTX + qb * P:CTX + (qb + 1) * P], Z[r, base + 4 + h // 2, XT])])

                attention(b2_units, score, lambda k, h, values=values: values[:, 2 + k, h * VD:(h + 1) * VD], QB[:, 0:2, :])
            pe.wait_ge(z_ready, n.next(z_ready))
            columns_loop(PLAN["attn_out"], 4, YB, slice(0, SEQ))
            norm_sum([range(KT)], XT)
            ffn(0)
            pre_norm()
            columns_loop(PLAN["rg_in"], 8, XN, XT)
            pe.wait_ge(z_ready, n.next(z_ready))
            for i in range(2):
                p = PLAN["rg_ai"] + i
                panel_wait(p)
                for half in range(2):
                    for b in range(4):
                        m = 4 * half + b
                        last = product(g_bank()[:, 0:SEQ], [(tile(p, 2 * m + k), XN[:, 2 * (m // 2) + k, XT]) for k in range(2)])
                    last.then_inc(halves_done, 1)
            pe.wait_ge(z_ready, n.next(z_ready))
            columns_loop(PLAN["rg_out"], 4, YB, slice(0, SEQ))
            norm_sum([range(KT)], XT)
            ffn(1)

        @block.scalar
        def _(act):
            n = Count()
            blocks = Count()
            A = nc.scalar.activation

            def link(ins):
                ins.then_inc(act_step, 1)
                act.wait_ge(act_step, n.next(act_step))

            def s_bank():
                b = n.next(s_ready)
                act.wait_ge(s_ready, b)
                return S[(b - 1) % 2]

            def halves(k):
                act.wait_ge(halves_done, k)

            def rstd(width, t, out):
                bank = s_bank()
                w = t.stop - t.start
                A(out[:, 0:w], bank[:, 0:w], ACT.Ln, bias=EPS, scale=1.0 / width).then_inc(s_free, 1)
                act.wait_ge(s_free, n.next(s_free))
                A(out[:, 0:w], out[:, 0:w], ACT.Exp, scale=-0.5).then_inc(rstd_ready, 1)

            def square(src, t):
                for k in range(0, KT, 2):
                    A(SQ[:, k:k + 2, t], src[:, k:k + 2, t], ACT.Square).then_inc(sq_ready, 1)

            def copies_loop(p0, panels, out, t, dst=None):
                base = blocks.at(g_free)
                dst = dst or t
                with act.Fori(0, panels // SLOTS) as g:
                    for i in range(2 * SLOTS):
                        act.wait_ge(halves_done, g * (2 * SLOTS) + (2 * p0 + i + 1))
                        o = out(g * (2 * SLOTS) + i, dst)
                        A(o, G[(base + i) % 4][:, 0:t.stop - t.start], ACT.Copy).then_inc(g_free, 1)
                blocks.next(g_free, 2 * panels)

            def g_next():
                return G[(blocks.next(g_free) - 1) % 4]

            def row(buf, off=0):
                return lambda i, t: buf[:, bass.ds(i + off, 1), t].rearrange("p a t -> p (a t)")

            def keys_on_partitions(i, nk, pt):
                act.wait_ge(turned, n.next(turned))
                if i >= 2:
                    act.wait_ge(pv_done, n.at(pv_done) - 1)
                A(pt[:, i % 2, 0:nk], DB[i % 2][:, 0:nk], ACT.Copy).then_inc(pt_ready, 1)
                n.next(pv_done)

            def softmax_units(units, source, pt):
                def exponentials(i):
                    nk = units[i][2]
                    b = n.next(s_ready)
                    n.next(s_free)
                    if source is None:
                        act.wait_ge(s_ready, b)
                        src = S[(b - 1) % 2][:, 0:nk]
                    else:
                        src = source(i)[:, 0:nk]
                    act.wait_ge(rowmax_ready, n.next(rowmax_ready))
                    A(PR[:, i % 2, 0:nk], src, ACT.Exp, bias=STAT[:, i % 2, 0:1],
                      accum_out=STAT[:, i % 2, 1:2]).then_inc(prob_ready, 1)

                for i in range(-1, len(units)):
                    if i + 1 < len(units):
                        exponentials(i + 1)
                    if i >= 0:
                        keys_on_partitions(i, units[i][2], pt)

            EPS = V[:, NVEC - 1:NVEC]
            act.wait_ge(const_in, 32)
            A(V[:, VEC["c"]:VEC["c"] + 2 * KT], V[:, VEC["c"]:VEC["c"] + 2 * KT], ACT.Silu).then_inc(silu_c_ready, 1)
            lam = V[:, VEC["lam"]:VEC["lam"] + KT]
            link(A(LT[:, 0, :], lam, ACT.Abs))
            link(A(LT[:, 0, :], LT[:, 0, :], ACT.Exp, scale=-1.0))
            A(LT[:, 0, :], LT[:, 0, :], ACT.Ln, bias=1.0).then_inc(soft_ready, 1)
            act.wait_ge(x_in, 16)

            def first_block(l):
                t = AT_ if l == 0 else XT
                blocks.next(g_free, 7)
                if l > 0:
                    act.wait_ge(layer_done, n.next(layer_done))
                square(X, AT_)
                rstd(D, AT_, RA)
                p0 = PLAN["win", l]
                for i in range(8):
                    halves(2 * p0 + i + 1)
                    A(Z[:, i, :], g_next()[:, :], ACT.Copy).then_inc(g_free, 1)
                copies_loop(p0 + 4, 8, row(Z, 8), slice(0, t.stop - t.start), t)
                act.wait_ge(g_free, blocks.at(g_free))
                blocks.next(g_free, 8)
                A(SQ[:, 0, :], Z[:, Z_KV, :], ACT.Square).then_inc(sq_ready, 1)
                A(SQ[:, 2:4, :], Z[:, Z_QLAT:Z_QLAT + 2, :], ACT.Square).then_inc(sq_ready, 1)
                A(Z[:, Z_GATE:, t], Z[:, Z_GATE:, t], ACT.Silu).then_inc(gates_ready, 1)
                rstd(KVR, AT_, RA)
                rstd(QR, AT_, PR[:, 0, :])
                act.wait_ge(kr_ready, n.next(kr_ready))
                A(KB[KR:KR + ROPE, :, :], Z[KR:KR + ROPE, Z_MISC, :].unsqueeze(1).to_broadcast([ROPE, HEADS, TOK]),
                  ACT.Copy).then_inc(kr_copied, 1)
                softmax_units(mla_units(l), None, Z[:, Z_QLAT:Z_QLAT + 2, :])
                blocks.next(g_free, 4)
                act.wait_ge(logit_ready, n.next(logit_ready))
                link(A(EX, LG, ACT.Abs))
                link(A(EX, EX, ACT.Exp, scale=-1.0))
                A(EX, EX, ACT.Ln, bias=1.0).then_inc(soft_ready, 1)
                for d in range(2):
                    r = slice(2 * d, 2 * d + 2)
                    act.wait_ge(expo_ready, n.next(expo_ready))
                    A(EE[:, 0:2, :], EX[:, 0:2, :], ACT.Exp, scale=1.0 / 16).then_inc(exp_ready, 1)
                    A(EE[:, 2:4, :], EX[:, 0:2, :], ACT.Exp, scale=-1.0 / 16).then_inc(exp_ready, 1)
                    act.wait_ge(expo_ready, n.next(expo_ready))
                    A(EE[:, 0:2, :], EX[:, 2:4, :], ACT.Exp, scale=1.0 / 16).then_inc(exp_ready, 1)
                    A(LG[:, r, :], LG[:, r, :], ACT.Exp, scale=1.0 / 16).then_inc(exp_ready, 1)
                blocks.next(g_free, 4)
                act.wait_ge(og_ready, n.next(og_ready))
                for h in range(GH):
                    A(SQ[:, h, t], OG[:, h, t], ACT.Square).then_inc(sq_ready, 1)
                for h in range(GH):
                    w = t.stop - t.start
                    bank = s_bank()
                    A(SQ[:, 4 + h, t], bank[:, 0:w], ACT.Ln, bias=EPS, scale=1.0 / GDV).then_inc(s_free, 1)
                    act.wait_ge(s_free, n.next(s_free))
                    A(SQ[:, 4 + h, t], SQ[:, 4 + h, t], ACT.Exp, scale=-0.5).then_inc(rstd_ready, 1)
                act.wait_ge(gla_done, n.next(gla_done))
                p0 = PLAN["merge", l]
                for b in range(3):
                    if b > 0:
                        act.wait_ge(merged_ready, n.next(merged_ready))
                    for i in range(8):
                        halves(2 * (p0 + 6 * b) + i + 1)
                        A(QB[:, i, t], g_next()[:, 0:t.stop - t.start], ACT.Sigmoid).then_inc(g_free, 1)
                    blocks.next(g_free, 8)
                n.next(merged_ready)
                copies_loop(PLAN["wout", l], 4, row(XN), t if l == 0 else slice(0, SEQ), t)
                act.wait_ge(g_free, blocks.at(g_free))
                square(XN, t)
                rstd(D, t, RA)

            def pre_norm():
                act.wait_ge(layer_done, n.next(layer_done))
                square(X, XT)
                rstd(D, XT, RA)

            def post_norm(wait=True):
                if wait:
                    act.wait_ge(g_free, blocks.at(g_free))
                square(XN, XT)
                rstd(D, XT, RA)

            def ffn(i):
                pre_norm()
                p0 = PLAN[f"gate_up{i}"]
                base = blocks.at(g_free)
                with act.Fori(0, 5) as g:
                    for u in range(SLOTS):
                        act.wait_ge(halves_done, g * (2 * SLOTS) + (2 * (p0 + u) + 1))
                        act.wait_ge(g_free, g * (2 * SLOTS) + (base + 2 * u - 2))
                        A(PR[:, u % 2, 0:SEQ], G[(base + 2 * u) % 4][:, 0:SEQ], ACT.Silu).then_inc(silu_ready, 1)
                for u in range(20, 22):
                    act.wait_ge(halves_done, 2 * (p0 + u) + 1)
                    act.wait_ge(g_free, base + 2 * u - 2)
                    A(PR[:, u % 2, 0:SEQ], G[(base + 2 * u) % 4][:, 0:SEQ], ACT.Silu).then_inc(silu_ready, 1)
                blocks.next(g_free, 44 + 4)
                act.wait_ge(block_ready, n.next(block_ready))
                post_norm(False)

            for l in range(DEPTH):
                first_block(l)
            pre_norm()
            copies_loop(PLAN["attn_qk"], 8, row(Z), slice(0, SEQ), XT)
            blocks.next(g_free, 8)
            softmax_units(b2_units, lambda i: SQ[:, i % 2, :], QB[:, 0:2, :])
            blocks.next(g_free, 4)

            def soft_part(i):
                bank = s_bank()
                n.next(s_free)
                T = SQ[:, i % 2, 0:SEQ]
                if i >= 2:
                    act.wait_ge(rowmax_ready, n.at(rowmax_ready) + i - 1)
                link(A(T, bank[:, 0:SEQ], ACT.Abs))
                link(A(T, T, ACT.Exp, scale=-1.0))
                A(T, T, ACT.Ln, bias=1.0).then_inc(soft_ready, 1)

            def weight_part(i):
                act.wait_ge(rowmax_ready, n.at(rowmax_ready) + i + 1)
                A(PR[:, i % 2, 0:SEQ], SQ[:, 4 + i % 2, 0:SEQ], ACT.Exp).then_inc(probn_ready, 1)

            for i in range(-2, len(b2_units)):
                if i + 2 < len(b2_units):
                    soft_part(i + 2)
                if 0 <= i + 1 < len(b2_units):
                    weight_part(i + 1)
                if i >= 0:
                    keys_on_partitions(i, SEQ, QB[:, 0:2, :])
            n.next(rowmax_ready, len(b2_units))
            blocks.next(g_free, 4)
            copies_loop(PLAN["attn_out"], 4, row(XN), slice(0, SEQ), XT)
            post_norm()
            ffn(0)
            pre_norm()
            copies_loop(PLAN["rg_in"], 8, row(Z), slice(0, SEQ), XT)
            act.wait_ge(g_free, blocks.at(g_free))
            A(Z[:, 0:8, XT], Z[:, 0:8, XT], ACT.Gelu_apprx_tanh).then_inc(gates_ready, 1)
            n.next(z_ready)
            p0 = PLAN["rg_ai"]
            for i, (dst, b) in enumerate(((QB, "ba"), (KB, "bi"))):
                for half in range(2):
                    halves(2 * (p0 + i) + half + 1)
                    for m in range(4 * half, 4 * half + 4):
                        A(dst[:, m, XT], g_next()[:, 0:SEQ], ACT.Sigmoid, bias=vec(b, m)).then_inc(g_free, 1)
            act.wait_ge(log_a_ready, 1)
            A(QB[:, :, XT], QB[:, :, CT], ACT.Exp).then_inc(exp_ready, 1)
            A(SQ[:, :, CT], QB[:, :, CT], ACT.Tanh, scale=-1.0).then_inc(exp_ready, 1)
            A(SQ[:, :, XT], QB[:, :, CT], ACT.Exp, scale=2.0).then_inc(exp_ready, 1)
            act.wait_ge(log_a_ready, 2)
            A(SQ[:, :, CT], SQ[:, :, CT], ACT.Sqrt).then_inc(exp_ready, 1)
            copies_loop(PLAN["rg_out"], 4, row(XN), slice(0, SEQ), XT)
            post_norm()
            ffn(1)

        @block.vector
        def _(dve):
            n = Count()
            blocks = Count()
            v = nc.vector

            def link(ins):
                ins.then_inc(dve_step, 1)
                dve.wait_ge(dve_step, n.next(dve_step))

            def d_bank():
                b = n.next(d_ready)
                dve.wait_ge(d_ready, b)
                return DB[(b - 1) % 2]

            def s_bank():
                b = n.next(s_ready)
                dve.wait_ge(s_ready, b)
                return S[(b - 1) % 2]

            def g_next():
                return G[(blocks.next(g_free) - 1) % 4]

            def wait(s, k=1):
                dve.wait_ge(s, n.next(s, k))

            def skip_s(k=1):
                n.next(s_ready, k)
                n.next(s_free, k)

            def segs(l):
                return (CT, XT) if l == 0 else (XT,)

            def gv_copies(p0, dsts, tbs):
                dve.wait_ge(g_free, blocks.at(g_free))
                for i, (dst, col) in enumerate(dsts):
                    for j, tb in enumerate(tbs):
                        if j < len(tbs) - 1:
                            wait(g_ready)
                        else:
                            dve.wait_ge(halves_done, 2 * (p0 + i) + 2)
                        last = v.tensor_copy(dst[:, tb, col:col + 256], g_next()[:, 0:256])
                        last.then_inc(g_free, 1)

            def add_normed(t_segs, gain):
                wait(rstd_ready)
                skip_s()
                off = t_segs[0].start
                for t in t_segs:
                    for k in range(KT):
                        r = RA[:, t.start - off:t.stop - off]
                        last = v.scalar_tensor_tensor(out=XN[:, k, t], in0=XN[:, k, t], scalar=gain(k, t), in1=r,
                                                      op0=ALU.mult, op1=ALU.mult)
                link(last)
                for t in t_segs:
                    last = v.tensor_tensor(X[:, :, t], X[:, :, t], XN[:, :, t], ALU.add)
                last.then_inc(layer_done, 1)
                dve.wait_ge(layer_done, n.next(layer_done))

            def plain_norm(gain):
                wait(rstd_ready)
                skip_s()
                for k in range(KT):
                    last = v.scalar_tensor_tensor(out=XN[:, k, XT], in0=X[:, k, XT], scalar=gain(k), in1=RA[:, 0:SEQ],
                                                  op0=ALU.mult, op1=ALU.mult)
                last.then_inc(xn_ready, 1)

            def out_of_bank(units, i, out):
                first_qb, last_qb = units[0][1], units[-1][1]
                if i >= 0:
                    n.next(pv_done)
                    h, qb, _ = units[i]
                    if h % 2 == 1 and qb == last_qb:
                        dve.wait_ge(pv_done, n.at(pv_done))
                        out(h // 2, g_next()[:, 0:(last_qb - first_qb + 1) * P])

            def softmax_units(units, rel, out):
                def front(i):
                    h, qb, nk = units[i]
                    bank = s_bank()
                    n.next(s_free)
                    if rel:
                        s = SQ[:, i % 2, 0:nk]
                        v.tensor_tensor(s, bank[:, 0:nk], BT[:, 2 * h + qb, :], ALU.add).then_inc(s_free, 1)
                        dve.wait_ge(s_free, n.at(s_free))
                    else:
                        s = bank[:, 0:nk]
                    v.tensor_reduce(STAT[:, i % 2, 0:1], s, AX, ALU.max, negate=True).then_inc(rowmax_ready, 1)

                def back(i):
                    st, p = STAT[:, i % 2, :], PR[:, i % 2, 0:units[i][2]]
                    wait(prob_ready)
                    if rel:
                        link(v.reciprocal(st[:, 2:3], st[:, 1:2]))
                    else:
                        v.reciprocal(st[:, 2:3], st[:, 1:2]).then_inc(s_free, 1)
                        dve.wait_ge(s_free, n.at(s_free) - (1 if i + 1 < len(units) else 0))
                    v.tensor_scalar(p, p, st[:, 2:3], None, ALU.mult).then_inc(probn_ready, 1)
                    n.next(probn_ready)

                for i in range(-1, len(units)):
                    if i + 1 < len(units):
                        front(i + 1)
                    if i >= 0:
                        back(i)
                        out_of_bank(units, i - 2, out)
                for i in (len(units) - 2, len(units) - 1):
                    out_of_bank(units, i, out)

            dve.wait_ge(const_in, 32)
            wait(soft_ready)
            lam = V[:, VEC["lam"]:VEC["lam"] + KT]
            link(v.tensor_scalar(LT[:, 1, :], lam, -1.0, 0.0, ALU.mult, ALU.max))
            link(v.tensor_tensor(LT[:, 1, :], LT[:, 1, :], LT[:, 0, :], ALU.add))
            link(v.tensor_scalar(NLAM[:, :], LT[:, 1, :], -8.0, None, ALU.mult))

            def first_block(l):
                t = AT_ if l == 0 else XT
                w = t.stop - t.start
                p0 = PLAN["mod", l]
                for c in range(6):
                    dve.wait_ge(halves_done, 2 * (p0 + 2 * c + 2))
                    v.tensor_copy(MROW[0:2, c * 512:(c + 1) * 512], g_next()[0:2, :]).then_inc(g_free, 1)
                dve.wait_ge(g_free, blocks.at(g_free))
                dve.sem_inc(modrow_ready, 1)
                wait(g_ready)
                b0 = VEC["mod_b"] + l * 6 * KT
                v.tensor_tensor(MOD[:, :, :], g_next()[:, 0:6 * KT].rearrange("p (a b) -> p a b", b=2),
                                V[:, b0:b0 + 6 * KT].rearrange("p (a b) -> p a b", b=2), ALU.add).then_inc(g_free, 1)
                dve.wait_ge(g_free, blocks.at(g_free))

                def both(name):
                    b = VEC[name] + l * KT
                    return V[:, b:b + KT].unsqueeze(2).to_broadcast([P, KT, 2])

                v.scalar_tensor_tensor(out=AMOD[:, :, :], in0=MOD[:, KT:2 * KT, :], scalar=1.0, in1=both("pre"),
                                       op0=ALU.add, op1=ALU.mult)
                link(v.tensor_tensor(GPOST[:, :, :], MOD[:, 2 * KT:, :], both("post"), ALU.mult))
                wait(rstd_ready)
                skip_s()
                for k in range(KT):
                    for s in (CT, XT):
                        e = seg(s)
                        last = v.scalar_tensor_tensor(out=XN[:, k, s], in0=X[:, k, s], scalar=AMOD[:, k, e:e + 1],
                                                      in1=RA[:, s], op0=ALU.mult, op1=ALU.mult)
                link(last)
                for k in range(KT):
                    for s in (CT, XT):
                        e = seg(s)
                        last = v.tensor_scalar(XN[:, k, s], XN[:, k, s], MOD[:, k, e:e + 1], None, ALU.add)
                last.then_inc(xn_ready, 1)
                blocks.next(g_free, 24)
                gv_copies(PLAN["gv", l], ((VG, 0), (VG, 256)), range(4))
                skip_s(2)
                wait(rstd_ready)
                v.scalar_tensor_tensor(out=Z[:, Z_KV, :], in0=Z[:, Z_KV, :], scalar=vec("kvn", l), in1=RA[:, :],
                                       op0=ALU.mult, op1=ALU.mult)
                wait(rstd_ready)
                for k in range(2):
                    last = v.scalar_tensor_tensor(out=Z[:, Z_QLAT + k, :], in0=Z[:, Z_QLAT + k, :],
                                                  scalar=vec("qn", 2 * l + k), in1=PR[:, 0, :], op0=ALU.mult, op1=ALU.mult)
                last.then_inc(lat_ready, 1)
                for h in range(HEADS):
                    v.tensor_scalar(QB[0:QKD, h, t], d_bank()[0:QKD, 0:w], float(QKD) ** -0.5, None, ALU.mult).then_inc(d_free, 1)
                dve.wait_ge(d_free, n.at(d_ready))
                dve.sem_inc(qcopy_ready, 1)
                for h in range(HEADS):
                    v.tensor_copy(KB[0:NOPE, h, :], d_bank()[0:NOPE, :]).then_inc(d_free, 1)
                for tb in range(4):
                    v.tensor_copy(VM[:, tb, :], d_bank()[:, :]).then_inc(d_free, 1)
                r = slice(KR, KR + ROPE)
                cos, sin = C[r, C_COS:C_COS + SEQ], C[r, C_SIN:C_SIN + SEQ]
                tmp = SQ[r, 4:6, 0:SEQ]
                v.tensor_tensor(tmp[:, 0, :], d_bank()[r, 0:SEQ], sin, ALU.mult).then_inc(d_free, 1)
                link(v.tensor_tensor(Z[r, Z_MISC, XT], Z[r, Z_MISC, XT], cos, ALU.mult))
                v.tensor_tensor(Z[r, Z_MISC, XT], Z[r, Z_MISC, XT], tmp[:, 0, :], ALU.add).then_inc(kr_ready, 1)
                dve.wait_ge(kr_ready, n.next(kr_ready))
                for h in range(0, HEADS, 2):
                    q = QB[r, h:h + 2, XT]
                    v.tensor_tensor(tmp, d_bank()[r, :].rearrange("p (h t) -> p h t", h=2),
                                    sin.unsqueeze(1).to_broadcast([ROPE, 2, SEQ]), ALU.mult).then_inc(d_free, 1)
                    link(v.tensor_tensor(q, q, cos.unsqueeze(1).to_broadcast([ROPE, 2, SEQ]), ALU.mult))
                    last = v.tensor_tensor(q, q, tmp, ALU.add)
                    if h < HEADS - 2:
                        link(last)
                last.then_inc(qkv_ready, 1)
                wait(gates_ready)

                def gated(j, o):
                    v.tensor_tensor(Z[:, Z_GATE + j, t], o, Z[:, Z_GATE + j, t], ALU.mult).then_inc(g_free, 1)

                softmax_units(mla_units(l), False, gated)
                for s in segs(l):
                    for g in range(4):
                        v.memset(CS[:, g, 0:PADW + 1], 0.0)
                        last = v.tensor_tensor_scan(CS[:, g, PADW + 1:PADW + 1 + SEQ], ones, Z[:, Z_POOL + g, s], 0.0,
                                                    ALU.mult, ALU.add)
                    link(last)
                    link(v.tensor_copy(CS[:, :, PADW + 1 + SEQ:], CS[:, :, PADW + SEQ:PADW + SEQ + 1]
                                       .to_broadcast([P, 4, PADW - 1])))
                    for g, win in enumerate(WINDOWS):
                        hi, lo = PADW + win // 2, PADW - win // 2
                        last = v.tensor_tensor(PB[:, g, s], CS[:, g, hi:hi + SEQ], CS[:, g, lo:lo + SEQ], ALU.subtract)
                    link(last)
                    edge = C[:, C_EDGE:C_EDGE + 8 * PADW].rearrange("p (g e t) -> p g e t", g=4, e=2)
                    for e, cols in enumerate((slice(s.start, s.start + PADW), slice(s.stop - PADW, s.stop))):
                        last = v.tensor_tensor(PB[:, :, cols], PB[:, :, cols], edge[:, :, e, :], ALU.mult)
                    link(last)
                    for g, win in enumerate(WINDOWS):
                        last = v.scalar_tensor_tensor(out=PB[:, g, s], in0=PB[:, g, s], scalar=1.0 / win,
                                                      in1=Z[:, Z_POOL + g, s], op0=ALU.mult, op1=ALU.subtract)
                    if s is not segs(l)[-1]:
                        link(last)
                last.then_inc(pooled_ready, 1)
                for g in range(4):
                    gate = Z[:, Z_GATE + 4 + g, t]
                    v.scalar_tensor_tensor(out=gate, in0=d_bank()[:, 0:w], scalar=vec("pscale", 4 * l + g), in1=gate,
                                           op0=ALU.mult, op1=ALU.mult).then_inc(d_free, 1)
                for i in range(4):
                    last = v.tensor_scalar(LG[:, i, :], d_bank()[:, :], vec("gab", 4 * l + i), None, ALU.add)
                    last.then_inc(d_free, 1)
                dve.wait_ge(d_free, n.at(d_ready))
                dve.sem_inc(logit_ready, 1)
                wait(soft_ready)
                link(v.scalar_tensor_tensor(out=EE, in0=LG, scalar=0.0, in1=EX, op0=ALU.min, op1=ALU.subtract))
                for d in range(2):
                    for j in range(2):
                        for c in range(NCH):
                            a = slice(c * GCH, (c + 1) * GCH) if d == 0 else (
                                slice((c + 1) * GCH - 1, c * GCH - 1 if c else None, -1))
                            last = v.tensor_tensor_scan(LG[:, 2 * d + j, a], ones[:, 0:GCH], EE[:, 2 * d + j, a], 0.0,
                                                        ALU.mult, ALU.add)
                link(last)
                for d in range(2):
                    r = slice(2 * d, 2 * d + 2)
                    mid, end = (GCH // 2 - 1, GCH - 1) if d == 0 else (GCH // 2, 0)
                    b = LG[:, r, :].rearrange("p j (c t) -> p (j c) t", t=GCH)
                    x0 = EX[:, 0:2, :].rearrange("p j (c t) -> p (j c) t", t=GCH)
                    x1 = EX[:, 2:4, :].rearrange("p j (c t) -> p (j c) t", t=GCH)
                    link(v.tensor_tensor(x0, b, b[:, :, mid:mid + 1].to_broadcast([P, 2 * NCH, GCH]), ALU.subtract))
                    v.tensor_scalar(EX[:, 0:2, :], EX[:, 0:2, :], -16 * CLAMP, 16 * CLAMP, ALU.max, ALU.min).then_inc(expo_ready, 1)
                    wait(exp_ready, 2)
                    q, k = Z[:, Z_GQ:Z_GQ + 2, :], Z[:, Z_GK:Z_GK + 2, :]
                    fl = lambda a: a.rearrange("p j t -> p (j t)")
                    v.scalar_tensor_tensor(out=QTB[:, r, :], in0=EE[:, 0:2, :], scalar=GDK ** -0.5, in1=q, op0=ALU.mult, op1=ALU.mult)
                    v.tensor_tensor(KTB[:, r, :], EE[:, 2:4, :], k, ALU.mult)
                    v.tensor_tensor(x1, b[:, :, end:end + 1].to_broadcast([P, 2 * NCH, GCH]), b, ALU.subtract).then_inc(expo_ready, 1)
                    wait(exp_ready, 2)
                    v.scalar_tensor_tensor(out=QEB[:, r, :], in0=LG[:, r, :], scalar=GDK ** -0.5, in1=q, op0=ALU.mult, op1=ALU.mult)
                    v.tensor_tensor(KDB[:, r, :], EE[:, 0:2, :], k, ALU.mult).then_inc(decayed, 1)
                    dve.wait_ge(decayed, n.next(decayed))
                for i in range(4):
                    v.tensor_copy(KDT[:, i * NCH:(i + 1) * NCH, :], d_bank()[:, :].rearrange("p (a b) -> p a b", b=P)).then_inc(d_free, 1)
                dve.wait_ge(d_free, n.at(d_ready))
                dve.sem_inc(kdt_ready, 1)
                for step in range(3):
                    bank = d_bank()
                    if step == 0:
                        last = v.tensor_copy(ST[0], bank[:, :])
                    else:
                        for d in range(2):
                            c = order[d][step]
                            end = c * GCH + (GCH - 1 if d == 0 else 0)
                            for j in range(2):
                                i = 2 * d + j
                                last = v.scalar_tensor_tensor(out=ST[step][:, i * P:(i + 1) * P], in0=ST[step - 1][:, i * P:(i + 1) * P],
                                                              scalar=LG[:, i, end:end + 1], in1=bank[:, i * P:(i + 1) * P],
                                                              op0=ALU.mult, op1=ALU.add)
                    last.then_inc(d_free, 1)
                    dve.wait_ge(d_free, n.at(d_ready))
                dve.sem_inc(state_ready, 1)
                first = 0 if l == 0 else 2
                mask = C[:, C_MASK:C_MASK + 256]
                for j in range(2):
                    for c in range(first, NCH):
                        i = n.next(gatt_ready, 2) // 2
                        for e in range(2):
                            bank = d_bank()
                            v.scalar_tensor_tensor(out=gatt(i)[:, 2 * e:2 * e + 2, :].rearrange("p a b -> p (a b)"),
                                                   in0=bank[:, 0:256], scalar=3.0e38, in1=mask,
                                                   op0=ALU.min, op1=ALU.mult).then_inc(gatt_ready, 1)
                            dve.wait_ge(gatt_ready, n.at(gatt_ready) - 1 + e)
                            dve.sem_inc(d_free, 1)
                    wait(g_ready, NCH - first)
                    for e in range(2):
                        last = v.tensor_copy(OG[:, 2 * j + e, t], g_next()[:, 0:w])
                        last.then_inc(g_free, 1)
                dve.wait_ge(g_free, blocks.at(g_free))
                dve.sem_inc(og_ready, 1)
                skip_s(4)
                for h in range(GH):
                    wait(rstd_ready)
                    last = v.scalar_tensor_tensor(out=OG[:, h, t], in0=OG[:, h, t], scalar=vec("gn", l), in1=SQ[:, 4 + h, t],
                                                  op0=ALU.mult, op1=ALU.mult)
                link(last)
                v.tensor_tensor(Z[:, Z_GATE + 8:, t], Z[:, Z_GATE + 8:, t], OG[:, :, t], ALU.mult).then_inc(gla_done, 1)
                p0 = PLAN["merge", l]
                for b in range(3):
                    blocks.next(g_free, 8)
                    for half in range(4):
                        dve.wait_ge(halves_done, 2 * (p0 + 6 * b + 4) + half + 1)
                        if half == 0:
                            dve.wait_ge(g_free, blocks.at(g_free))
                        for i in (2 * half, 2 * half + 1):
                            bank = g_next()[:, 0:w]
                            if b == 0:
                                last = v.tensor_tensor(KB[:, i, t], bank, QB[:, i, t], ALU.mult)
                            else:
                                last = v.tensor_tensor(QB[:, i, t], bank, QB[:, i, t], ALU.mult)
                            last.then_inc(g_free, 1)
                    dve.wait_ge(g_free, blocks.at(g_free))
                    m = n.next(merged_ready)
                    if b == 0:
                        dve.sem_inc(merged_ready, 1)
                    else:
                        v.tensor_tensor(KB[:, :, t], KB[:, :, t], QB[:, :, t], ALU.add).then_inc(merged_ready, 1)
                        dve.wait_ge(merged_ready, m)
                blocks.next(g_free, 8)
                add_normed(segs(l), lambda k, s: GPOST[:, k, seg(s):seg(s) + 1])

            def ffn(i):
                plain_norm(lambda k: vec("ffnpre", KT * i + k))
                p0 = PLAN[f"gate_up{i}"]
                base = blocks.at(g_free)
                with dve.Fori(0, 5) as g:
                    for u in range(SLOTS):
                        dve.wait_ge(silu_ready, g * SLOTS + (22 * i + u + 1))
                        dve.wait_ge(halves_done, g * (2 * SLOTS) + (2 * (p0 + u) + 2))
                        o = H[:, bass.ds(g * SLOTS + u, 1), :].rearrange("p a t -> p (a t)")
                        v.tensor_tensor(o, PR[:, u % 2, 0:SEQ], G[(base + 2 * u + 1) % 4][:, 0:SEQ], ALU.mult).then_inc(g_free, 2)
                for u in range(20, 22):
                    dve.wait_ge(silu_ready, 22 * i + u + 1)
                    dve.wait_ge(halves_done, 2 * (p0 + u) + 2)
                    v.tensor_tensor(H[:, u, :], PR[:, u % 2, 0:SEQ], G[(base + 2 * u + 1) % 4][:, 0:SEQ], ALU.mult).then_inc(g_free, 2)
                blocks.next(g_free, 44)
                dve.wait_ge(halves_done, 2 * (PLAN[f"down{i}"] + 11))
                banks = [g_next() for _ in range(4)] + [*S, *DB]
                for m in range(KT):
                    last = v.tensor_copy(XN[:, m, XT], banks[m][:, 0:SEQ])
                last.then_inc(g_free, 4)
                dve.wait_ge(g_free, blocks.at(g_free))
                dve.sem_inc(block_ready, 1)
                add_normed((XT,), lambda k, s: vec("ffnpost", KT * i + k))

            for l in range(DEPTH):
                first_block(l)
            dve.sem_inc(block1_free, 1)
            plain_norm(lambda k: vec("mixpre", k))
            blocks.next(g_free, 16)
            p0 = PLAN["attn_v"]
            gv_copies(p0, ((VG, 0), (VG, 256), (VM, 0), (VM, 256)), (2, 3))
            dve.wait_ge(g_free, blocks.at(g_free))
            v.tensor_scalar(Z[:, 0:4, XT], Z[:, 0:4, XT], 0.125, None, ALU.mult).then_inc(z_ready, 1)
            dve.wait_ge(bias_in, 32)
            bt4 = BT.rearrange("p (h q) t -> p h q t", q=2)
            for qb in range(2):
                last = v.tensor_tensor(bt4[:, :, qb, :], bt4[:, :, qb, :],
                                       causal_neg[:, qb, :].unsqueeze(1).to_broadcast([P, HEADS, SEQ]), ALU.add)
            link(last)
            v.tensor_scalar(Z[:, 8:12, XT], Z[:, 8:12, XT], 0.125, None, ALU.mult).then_inc(z_ready, 1)

            def copied(off):
                def out(j, o):
                    v.tensor_copy(YB[:, off + j, :], o).then_inc(g_free, 1)
                return out

            softmax_units(b2_units, True, copied(0))

            def sticks(i):
                h, qb, nk = b2_units[i]
                bank = s_bank()
                T, R = SQ[:, i % 2, 0:SEQ], SQ[:, 2 + i % 2, 0:SEQ]
                W = SQ[:, 4 + i % 2, 0:SEQ]
                wait(soft_ready)
                link(v.scalar_tensor_tensor(out=T, in0=bank[:, 0:SEQ], scalar=0.0, in1=T, op0=ALU.max, op1=ALU.add))
                link(v.tensor_tensor(T, T, strict[:, qb, :], ALU.mult))
                link(v.tensor_tensor_scan(R[:, ::-1], ones, T[:, ::-1], 0.0, ALU.mult, ALU.add))
                v.tensor_tensor(R, bank[:, 0:SEQ], R, ALU.subtract).then_inc(s_free, 1)
                dve.wait_ge(s_free, n.next(s_free))
                if i >= 2:
                    dve.wait_ge(probn_ready, n.at(probn_ready) + i - 1)
                v.tensor_tensor(W, R, strict_neg[:, qb, :], ALU.add).then_inc(rowmax_ready, 1)

            for i in range(len(b2_units)):
                sticks(i)
                out_of_bank(b2_units, i - 3, copied(4))
            for i in range(len(b2_units) - 3, len(b2_units)):
                out_of_bank(b2_units, i, copied(4))
            dve.wait_ge(g_free, blocks.at(g_free))
            dve.sem_inc(z_ready, 1)
            blocks.next(g_free, 8)
            add_normed((XT,), lambda k, s: vec("mixpost", k))
            ffn(0)
            plain_norm(lambda k: vec("mixpre", KT + k))
            blocks.next(g_free, 16)
            wait(gates_ready)
            for k in range(KT):
                last = v.tensor_scalar(XN[:, k, XT], Z[:, 8 + k, XT], vec("convw", 3 * KT + k), vec("convb", k), ALU.mult, ALU.add)
            for back in range(1, 4):
                link(last)
                for k in range(KT):
                    o = XN[:, k, CTX + back:TOK]
                    last = v.scalar_tensor_tensor(out=o, in0=Z[:, 8 + k, CTX:TOK - back], scalar=vec("convw", (3 - back) * KT + k),
                                                  in1=o, op0=ALU.mult, op1=ALU.add)
            last.then_inc(z_ready, 1)
            n.next(z_ready)
            blocks.next(g_free, 16)
            dve.wait_ge(g_free, blocks.at(g_free) - 8)
            for k in range(KT):
                last = v.tensor_scalar(QB[:, k, CT], QB[:, k, XT], NLAM[:, k:k + 1], None, ALU.mult)
            last.then_inc(log_a_ready, 1)
            wait(exp_ready, 3)
            v.scalar_tensor_tensor(out=SQ[:, :, CT], in0=SQ[:, :, XT], scalar=1.0, in1=SQ[:, :, CT],
                                   op0=ALU.add, op1=ALU.mult).then_inc(log_a_ready, 1)
            dve.wait_ge(g_free, blocks.at(g_free))
            link(v.tensor_tensor(KB[:, :, XT], KB[:, :, XT], XN[:, :, XT], ALU.mult))
            wait(exp_ready)
            link(v.tensor_tensor(KB[:, :, XT], KB[:, :, XT], SQ[:, :, CT], ALU.mult))
            for k in range(KT):
                last = v.tensor_tensor_scan(KB[:, k, CT], QB[:, k, XT], KB[:, k, XT], 0.0, ALU.mult, ALU.add)
            link(last)
            v.tensor_tensor(YB[:, :, :], KB[:, :, CT], Z[:, 0:8, XT], ALU.mult).then_inc(z_ready, 1)
            n.next(z_ready)
            blocks.next(g_free, 8)
            add_normed((XT,), lambda k, s: vec("mixpost", KT + k))
            ffn(1)


def constants():
    import numpy as np
    f = np.float32
    c = np.zeros((P, NCONST), f)
    c[:, C_ONES:C_ONES + 256] = 1
    c[:, C_ID:C_ID + P] = np.eye(P)
    key, query = np.arange(P)[:, None], np.arange(P)[None, :]
    c[:, C_MASK:C_MASK + P] = key <= query
    c[:, C_MASK + P:C_MASK + 2 * P] = key >= query
    inv = (f(10000.0) ** (-np.arange(0, ROPE // 2, 2, dtype=f) / f(ROPE // 2))).astype(f)
    t = np.arange(SEQ)
    ang = np.concatenate([(t // 64).astype(f)[None] * inv[:, None]] * 2 + [(t % 64).astype(f)[None] * inv[:, None]] * 2)
    c[KR:KR + ROPE, C_COS:C_COS + SEQ] = np.cos(ang)
    c[KR:KR + ROPE, C_SIN:C_SIN + SEQ] = np.sin(ang)
    for m in range(ROPE):
        c[KR + (m + 8 if m % 16 < 8 else m - 8), C_ROT + m] = -1 if m % 16 < 8 else 1
    for g, w in enumerate(WINDOWS):
        for e, ts in enumerate((np.arange(PADW), np.arange(SEQ - PADW, SEQ))):
            count = np.minimum(ts + w // 2, SEQ) - np.maximum(ts - w // 2, 0)
            at = C_EDGE + (2 * g + e) * PADW
            c[:, at:at + PADW] = w / count
    q = np.arange(SEQ).reshape(2, P).T[:, :, None]
    k = np.arange(SEQ)[None, None, :]
    c2 = np.concatenate([(k < q).astype(f), np.where(k < q, 0, -1e30).astype(f),
                         np.where(k // 64 <= q // 64, 0, -1e30).astype(f)], axis=1)
    return c, np.ascontiguousarray(c2)


def kernel(**inputs):
    import numpy as np
    import concourse.bacc as bacc
    from concourse.bass_utils import run_bass_kernel_spmd

    a = {n: np.asarray(x) for n, x in inputs.items()}
    ws = np.empty((PANELS, P, PANEL), np.float32)

    def put(at, x):
        ws[at:at + len(x)] = x.reshape(len(x), P, PANEL)

    def cols(w, per=2):
        k = w.shape[0] // P
        return w.reshape(k, P, -1, per, P).transpose(2, 1, 3, 0, 4)

    def rows(w):
        return w.reshape(KT, P, -1, 256).transpose(2, 1, 0, 3)

    ends = np.cumsum([0, QR, KVR, ROPE, 512, 512, 512, 256, 256, 512, 16, 16, 512, 3 * D])
    names = ("q", "kv", "kr", "mg", "px", "pg", "gq", "gk", "gv", "af", "ab", "gg", "merge")
    small = np.zeros((DEPTH, P, NSW), np.float32)
    for l in range(DEPTH):
        w = {n: a["w_in"][l][:, ends[i]:ends[i + 1]] for i, n in enumerate(names)}
        pad = np.zeros((D, 16), np.float32)
        win = np.concatenate([w["kv"], w["af"], pad, w["ab"], pad, w["kr"], pad, pad, w["gk"], w["gq"], w["q"],
                              w["px"], w["mg"], w["pg"], w["gg"]], axis=1)
        put(PLAN["mod", l], a["mod_w"][l].reshape(2, 4, P, 6, 512).transpose(3, 0, 2, 1, 4).reshape(12, P, -1))
        put(PLAN["win", l], cols(win))
        put(PLAN["gv", l], rows(w["gv"]))
        for b, branch in enumerate(("w_branch_mla", "w_branch_pool", "w_branch_gla")):
            put(PLAN["merge", l] + 6 * b, cols(w["merge"][:, b * D:(b + 1) * D]))
            put(PLAN["merge", l] + 6 * b + 4, cols(a[branch][l], 4))
        put(PLAN["wout", l], cols(a["w_out"][l]))
        small[l, :, SW_UQ:SW_UK] = a["mla_w_uq"][l].reshape(2, P, -1).transpose(1, 0, 2).reshape(P, -1)
        ukv = a["mla_w_ukv"][l].reshape(P, HEADS, NOPE + VD)
        small[l, :, SW_UK:SW_UV] = ukv[:, :, :NOPE].reshape(P, -1)
        small[l, :, SW_UV:SW_PW] = ukv[:, :, NOPE:].reshape(P, -1)
        small[l, :, SW_PW:SW_DW] = a["pool_w"][l].transpose(1, 0, 2).reshape(P, -1)
        small[l, AF:AF + 16, SW_DW:NSW] = a["gla_af_w2"][l]
        small[l, AB:AB + 16, SW_DW:NSW] = a["gla_ab_w2"][l]
    ain = a["attn_w_in_2"][0].reshape(D, 6, 512)
    put(PLAN["attn_qk"], cols(np.ascontiguousarray(ain[:, [0, 1, 3, 4]]).reshape(D, -1)))
    put(PLAN["attn_v"], rows(np.ascontiguousarray(ain[:, [2, 5]]).reshape(D, -1)))
    put(PLAN["attn_out"], cols(a["attn_w_out_2"][0]))
    put(PLAN["rg_in"], cols(a["rg_w_in_2"][0]))
    for i, n in enumerate(("rg_w_a_2", "rg_w_i_2")):
        put(PLAN["rg_ai"] + i, a[n][0].reshape(4, 2, P, 2, P).transpose(2, 0, 3, 1, 4)[None])
    put(PLAN["rg_out"], cols(a["rg_w_out_2"][0]))
    for i in range(2):
        gate, up = (cols(a[n][i], 1) for n in ("ffn_w_gate_2", "ffn_w_up_2"))
        put(PLAN[f"gate_up{i}"], np.concatenate([gate, up], axis=2))
        put(PLAN[f"down{i}"], a["ffn_w_down_2"][i].reshape(FB // 2, 2, P, KT, P).transpose(0, 2, 1, 3, 4))

    vecs = np.zeros((P, NVEC), np.float32)

    def column(name, x, at=0):
        x = x.reshape(-1, P).T
        vecs[:, VEC[name] + at:VEC[name] + at + x.shape[1]] = x

    both = np.stack([a["c_ctx"], a["c"][0]])
    vecs[:, VEC["c"]:VEC["c"] + 2 * KT] = both.reshape(2, KT, P).transpose(2, 1, 0).reshape(P, -1)
    vecs[:, VEC["mod_b"]:VEC["mod_b"] + DEPTH * 6 * KT] = np.repeat(a["mod_b"].reshape(-1, P).T, 2, axis=1)
    for name, n in (("pre", "pre_norm"), ("post", "post_norm"), ("qn", "mla_q_norm"), ("kvn", "mla_kv_norm"),
                    ("pscale", "pool_scale"), ("gn", "gla_norm"), ("mixpre", "norm_mix_pre_2"),
                    ("mixpost", "norm_mix_post_2"), ("ffnpre", "norm_ffn_pre_2"), ("ffnpost", "norm_ffn_post_2"),
                    ("convw", "rg_conv_w_2"), ("convb", "rg_conv_b_2"), ("ba", "rg_b_a_2"), ("bi", "rg_b_i_2"),
                    ("lam", "rg_lambda_2")):
        column(name, a[n])
    for l in range(DEPTH):
        column("gab", a["gla_af_b"][l], 4 * l)
        column("gab", a["gla_ab_b"][l], 4 * l + 2)
    vecs[:, VEC["eps"]] = NORM_EPS

    tokens = np.concatenate([a["ctx"][0], a["x"][0]])
    consts, consts2 = constants()
    q, k = np.arange(SEQ).reshape(2, P).T[:, :, None], np.arange(SEQ)[None, None, :]
    arrays = {
        "x_t": np.ascontiguousarray(tokens.reshape(TOK, KT, P).transpose(2, 1, 0)),
        "wstream": ws, "small": small, "vecs": vecs, "consts": consts,
        "rel": np.ascontiguousarray(a["attn_rel_bias_2"][0][:, q - k + SEQ].transpose(1, 0, 2, 3).reshape(P, 2 * HEADS, SEQ)),
        "consts2": consts2,
    }
    nc = bacc.Bacc("TRN2", target_bir_lowering=False, num_devices=1)
    args = [nc.dram_tensor(n, list(x.shape), mybir.dt.float32, kind="ExternalInput").ap() for n, x in arrays.items()]
    out = nc.dram_tensor("out_t", [P, KT, SEQ], mybir.dt.float32, kind="ExternalOutput").ap()
    program(nc, *args, out)
    r = run_bass_kernel_spmd(nc, [arrays], core_ids=[0])
    return np.asarray(r.results[0]["out_t"]).transpose(2, 1, 0).reshape(1, SEQ, D)
```

```python
import concourse.bass as bass
from concourse import mybir
from contextlib import ExitStack

P = 128
D = 1024
KT = D // P
SEQ, CTX = 256, 256
TOK = CTX + SEQ
DEPTH = 2
QR, KVR = 256, 128
HEADS, NOPE, ROPE, VD = 8, 64, 32, 64
QKD = NOPE + ROPE
GH, GDK, GDV, GCH = 4, 64, 128, 128
NCH = TOK // GCH
WINDOWS = (2, 4, 8, 16)
PADW = max(WINDOWS) // 2
DFF = 2816
FB = DFF // P
NORM_EPS = 1e-6
CLAMP = 80.0

SLOTS = 3
HALF = 8 * P
TURN = 12
PLAN = {}


def plan():
    at = 0
    for l in range(DEPTH):
        for name, n in (("mod", 12), ("win", 12), ("gv", 2), ("merge", 18), ("wout", 4)):
            PLAN[name, l] = at
            at += n
    for name, n in (("attn_qk", 8), ("attn_v", 4), ("attn_out", 4), ("gate_up0", 22), ("down0", 11),
                    ("rg_in", 8), ("rg_ai", 2), ("rg_out", 4), ("gate_up1", 22), ("down1", 11)):
        PLAN[name] = at
        at += n
    return at


HALVES = 2 * plan()

Z_KV, Z_MISC, Z_GK, Z_GQ, Z_QLAT, Z_POOL, Z_GATE = 0, 1, 2, 4, 6, 8, 12
AF, AB, KR = 0, 32, 64

VEC = {}


def vectors():
    at = 0
    for name, n in (("c", 2 * KT), ("mod_b", DEPTH * 2 * 3 * KT), ("pre", DEPTH * KT), ("post", DEPTH * KT),
                    ("qn", DEPTH * 2), ("kvn", DEPTH), ("pscale", DEPTH * 4), ("gab", DEPTH * 4), ("gn", DEPTH),
                    ("mixpre", DEPTH * KT), ("mixpost", DEPTH * KT), ("ffnpre", DEPTH * KT),
                    ("ffnpost", DEPTH * KT), ("convw", 4 * KT), ("convb", KT), ("ba", KT), ("bi", KT), ("lam", KT), ("eps", 1)):
        VEC[name] = at
        at += n
    return at


NVEC = vectors()
SW_UQ, SW_UK, SW_UV, SW_PW, SW_DW = 0, 1536, 2048, 2560, 3072
NSW = 3328
C_ONES, C_ID, C_MASK, C_COS, C_SIN, C_ROT, C_EDGE = 0, 256, 384, 640, 896, 1152, 1184
NCONST = C_EDGE + 4 * 2 * PADW


order = ([0, 1, 2, 3], [1, 0, 3, 2])


def mla_units(l):
    return [(h, qb, CTX if qb < 2 else TOK) for h in range(HEADS) for qb in range(0 if l == 0 else 2, 4)]


b2_units = [(h, qb, SEQ) for h in range(HEADS) for qb in range(2)]


def program(nc, x_t, wstream, small, vecs, consts, rel, consts2, out_t):
    f32 = mybir.dt.float32
    f32r = mybir.dt.float32r
    ALU = mybir.AluOpType
    ACT = mybir.ActivationFunctionType
    AX = mybir.AxisListType.X
    CT, XT, AT_ = slice(0, CTX), slice(CTX, TOK), slice(0, TOK)

    with ExitStack() as ctx:
        def sb(name, *shape, dt=f32, on=None):
            return (on or ctx).enter_context(nc.sbuf_tensor(name, [P, *shape], dt))

        def sem(name):
            return ctx.enter_context(nc.semaphore(name))

        RAW = sb("RAW", SLOTS, HALF)
        WH = sb("WH", SLOTS, HALF, dt=f32r)
        WL = sb("WL", SLOTS, HALF, dt=f32r)
        X = sb("X", KT, TOK)
        XN = sb("XN", KT, TOK)
        ZG = sb("ZG", 12, TOK)
        SQ = sb("SQ", KT, TOK)
        PR = sb("PR", 2, 512)
        RA = sb("RA", 512)
        V = sb("V", NVEC)
        C = sb("C", NCONST)
        MOD = sb("MOD", 3 * KT, 2)
        AMOD = sb("AMOD", KT, 2)
        GPOST = sb("GPOST", KT, 2)
        NLAM = sb("NLAM", KT)
        LT = sb("LT", 4, KT)
        STAT = sb("STAT", 2, 4)
        G = [ctx.enter_context(nc.psum_tensor(f"G{i}", [P, 512], f32)) for i in range(4)]
        S = [ctx.enter_context(nc.psum_tensor(f"S{i}", [P, 512], f32)) for i in range(2)]
        DB = [ctx.enter_context(nc.psum_tensor(f"D{i}", [P, 512], f32)) for i in range(2)]

        with ExitStack() as on:
            QB = sb("QB", KT, TOK, on=on)
            KB = sb("KB", KT, TOK, on=on)
        XH = sb("XH", KT, TOK, dt=f32r)
        XL = sb("XL", KT, TOK, dt=f32r)
        with ExitStack() as on:
            Z = sb("Z", 12, TOK, on=on)
            VG = sb("VG", 4, 512, on=on)
            VM = sb("VM", 4, 512, on=on)
            SW = sb("SW", NSW, on=on)
        with ExitStack() as on:
            SG = sb("SG", KT, TOK, on=on)
            MG = sb("MG", KT, TOK, on=on)
            YH = sb("YH", 4, TOK, dt=f32r, on=on)
            YL = sb("YL", 4, TOK, dt=f32r, on=on)
        with ExitStack() as on:
            Z2 = sb("Z2", 16, SEQ, on=on)
            BT = sb("BT", 16, SEQ, on=on)
            VA, VS = sb("VA", 2, 512, on=on), sb("VS", 2, 512, on=on)
            YB = sb("YB", KT, SEQ, on=on)
            PT2 = sb("PT2", 2, 512, on=on)
        with ExitStack() as on:
            Z3 = sb("Z3", 16, SEQ, on=on)
            QR_ = sb("QR", KT, TOK, on=on)
            KR_ = sb("KR", KT, TOK, on=on)
        with ExitStack() as on:
            HH = sb("HH", FB, SEQ, dt=f32r, on=on)
            HL = sb("HL", FB, SEQ, dt=f32r, on=on)

        def flat(t):
            return t[:, :, :].rearrange("p a b -> p (a b)")

        KDT = VM[:, :, :].rearrange("p a (b c) -> p (a b) c", c=P)
        LG = Z[:, Z_POOL:Z_POOL + 4, :]
        EX = SQ[:, 0:4, :]
        EE = SQ[:, 4:8, :]
        QTB, QEB = QB[:, 0:4, :], QB[:, 4:8, :]
        KTB, KDB = KB[:, 0:4, :], KB[:, 4:8, :]
        ST = [PR[:, 0, :], PR[:, 1, :], Z[:, Z_KV, :]]
        OG = Z[:, Z_GK:Z_GK + 4, :]
        CS = flat(SQ)[:, 0:4 * (SEQ + 2 * PADW)].rearrange("p (g t) -> p g t", g=4)
        PB = SQ[:, 4:8, :]
        MROW = flat(XN)[:, 0:3 * D]
        ones = C[:, C_ONES:C_ONES + 256]
        ident = C[:, C_ID:C_ID + P]
        strict, strict_neg, causal_neg = X[:, 0:2, CT], X[:, 2:4, CT], X[:, 4:6, CT]

        def gatt(i):
            return Z[:, Z_QLAT + i % 2, :].rearrange("p (a b) -> p a b", b=P)

        def c_rep(t):
            return t[:, 0:2, :].rearrange("p a (k r c) -> p (a k) r c", r=P // 2, c=2)

        def c_pairs():
            return V[:, VEC["c"]:VEC["c"] + 2 * KT].rearrange("p (k c) -> p k c", c=2).unsqueeze(2).to_broadcast([P, KT, P // 2, 2])

        def vec(name, i):
            return V[:, VEC[name] + i:VEC[name] + i + 1]

        def seg(t):
            return 1 if t is XT else 0

        raw_in = [sem(f"raw_in{i}") for i in range(SLOTS)]
        hi_ready, lo_ready = sem("hi_ready"), sem("lo_ready")
        xraw_ready, xh_ready = sem("xraw_ready"), sem("xh_ready")
        y_ready = sem("y_ready")
        hraw_ready, hh_ready, hl_ready = sem("hraw_ready"), sem("hh_ready"), sem("hl_ready")
        const_in, x_in, small_in, bias_in, out_done = sem("const_in"), sem("x_in"), sem("small_in"), sem("bias_in"), sem("out_done")
        halves_done = sem("halves_done")
        g_ready, g_free = sem("g_ready"), sem("g_free")
        s_ready, s_free = sem("s_ready"), sem("s_free")
        d_ready, d_free = sem("d_ready"), sem("d_free")
        dve_step, act_step = sem("dve_step"), sem("act_step")
        silu_c_ready, cl_ready, modrow_ready = sem("silu_c_ready"), sem("cl_ready"), sem("modrow_ready")
        sq_ready, rstd_ready, xn_ready = sem("sq_ready"), sem("rstd_ready"), sem("xn_ready")
        block_ready = sem("block_ready")
        z_ready, gates_ready = sem("z_ready"), sem("gates_ready")
        gv_ready, lat_ready, qkv_ready = sem("gv_ready"), sem("lat_ready"), sem("qkv_ready")
        qcopy_ready = sem("qcopy_ready")
        kr_ready, kr_copied = sem("kr_ready"), sem("kr_copied")
        turned, rowmax_ready, prob_ready, probn_ready, pt_ready, pv_done = (
            sem("turned"), sem("rowmax_ready"), sem("prob_ready"), sem("probn_ready"), sem("pt_ready"), sem("pv_done"))
        pooled_ready = sem("pooled_ready")
        logit_ready, soft_ready, expo_ready, exp_ready, decayed = (
            sem("logit_ready"), sem("soft_ready"), sem("expo_ready"), sem("exp_ready"), sem("decayed"))
        kdt_ready, state_ready, gatt_ready, og_ready = (
            sem("kdt_ready"), sem("state_ready"), sem("gatt_ready"), sem("og_ready"))
        gla_done = sem("gla_done")
        merged_ready, block1_free = sem("merged_ready"), sem("block1_free")
        silu_ready, log_a_ready = sem("silu_ready"), sem("log_a_ready")
        layer_done = sem("layer_done")

        block = ctx.enter_context(nc.Block())

        class Count:

            def __init__(self):
                self.n = {}

            def next(self, s, k=1):
                self.n[s.name] = self.n.get(s.name, 0) + k
                return self.n[s.name]

            def at(self, s):
                return self.n.get(s.name, 0)

        @block.sync
        def _(sp):
            sp.dma_start(V[:, :], vecs).then_inc(const_in, 16)
            sp.dma_start(C[:, :], consts).then_inc(const_in, 16)
            for s in range(SLOTS):
                sp.dma_start(RAW[:, s, :], wstream[s]).then_inc(raw_in[s], 16)
            sp.dma_start(X[:, :, :], x_t).then_inc(x_in, 16)
            with sp.Fori(0, HALVES // SLOTS - 1) as g:
                for s in range(SLOTS):
                    sp.wait_ge(lo_ready, g * SLOTS + (s + 1))
                    sp.dma_start(RAW[:, s, :], wstream[bass.ds(g * SLOTS + (s + SLOTS), 1), :, :]
                                 .rearrange("a p c -> (a p) c")).then_inc(raw_in[s], 16)
            sp.wait_ge(layer_done, 6)
            sp.dma_start(out_t, X[:, :, XT]).then_inc(out_done, 16)
            sp.wait_ge(out_done, 16)

        @block.gpsimd
        def _(pool):
            pool.dma_start(SW[:, :], small[0]).then_inc(small_in, 16)
            pool.wait_ge(layer_done, 1)
            pool.dma_start(SW[:, :], small[1]).then_inc(small_in, 16)
            pool.wait_ge(block1_free, 1)
            pool.dma_start(BT[:, :, :], rel).then_inc(bias_in, 16)
            pool.dma_start(X[:, 0:6, CT], consts2).then_inc(bias_in, 16)

            def hidden(i, f, g):
                def v(x, m):
                    return x if g is None else g * m + x

                raw = XN[:, f % 3, XT]
                hh = HH[:, f, :] if g is None else HH[:, bass.ds(g * (TURN // 2) + f, 1), :].rearrange("p a t -> p (a t)")
                hl = HL[:, f, :] if g is None else HL[:, bass.ds(g * (TURN // 2) + f, 1), :].rearrange("p a t -> p (a t)")
                pool.wait_ge(hraw_ready, v(FB * i + f + 1, TURN // 2))
                nc.gpsimd.tensor_copy(hh, raw).then_inc(hh_ready, 1)
                pool.wait_ge(hh_ready, v(FB * i + f + 1, TURN // 2))
                nc.gpsimd.tensor_tensor(hl, raw, hh.bitcast(f32), ALU.subtract).then_inc(hl_ready, 1)

            for i in range(2):
                with pool.Fori(0, 2 * FB // TURN) as g:
                    for f in range(TURN // 2):
                        hidden(i, f, g)
                for f in range(2 * FB // TURN * (TURN // 2), FB):
                    hidden(i, f, None)

        @block.tensor
        def _(pe):
            n = Count()
            blocks = Count()

            def product3(out, slot, terms):
                passes = [(w, a) for t, xh, xl in terms for w, a in ((WH, xh), (WH, xl), (WL, xh)) for w in [w[:, slot, t * P:(t + 1) * P]]]
                return product(out, passes)

            def g_bank():
                b = blocks.next(g_free) - 1
                if b >= 4:
                    pe.wait_ge(g_free, b - 3)
                return G[b % 4]

            def d_bank():
                b = n.next(d_ready) - 1
                if b >= 2:
                    pe.wait_ge(d_free, b - 1)
                return DB[b % 2]

            def s_bank():
                b = n.next(s_ready) - 1
                if b >= 2:
                    pe.wait_ge(s_free, b - 1)
                return S[b % 2]

            def product(out, pairs):
                for i, (w, x) in enumerate(pairs):
                    last = nc.tensor.matmul(out, w, x, start=i == 0, stop=i == len(pairs) - 1)
                return last

            def columns(k0, count, xh, xl, t, per_half=1, kts=KT, kt_of=lambda b, k: k):
                base = blocks.at(g_free)

                def body(i, g):
                    k = k0 + i
                    pe.wait_ge(lo_ready, k + 1 if g is None else g * TURN + (k + 1))
                    for b in range(per_half):
                        at = base + per_half * i + b
                        if g is not None:
                            pe.wait_ge(g_free, g * (TURN * per_half) + (at - 3))
                        elif at >= 4:
                            pe.wait_ge(g_free, at - 3)
                        last = product3(G[at % 4][:, 0:t.stop - t.start], k % SLOTS,
                                        [(b * kts + j, xh[:, kt_of(per_half * i + b, j), t], xl[:, kt_of(per_half * i + b, j), t])
                                         for j in range(kts)])
                    last.then_inc(halves_done, 1)

                if count >= TURN:
                    with pe.Fori(0, count // TURN) as g:
                        for i in range(TURN):
                            body(i, g)
                for i in range(count // TURN * TURN, count):
                    body(i, None)
                blocks.next(g_free, per_half * count)

            def token_rows(k0, xh, xl, tbs):
                banks = [g_bank() for _ in tbs]
                for half in range(2):
                    pe.wait_ge(lo_ready, k0 + half + 1)
                    s = (k0 + half) % SLOTS
                    for bank, tb in zip(banks, tbs):
                        for j in range(4):
                            kt, cols = 4 * half + j, slice(j * 256, (j + 1) * 256)
                            rows_ = slice(tb * P, (tb + 1) * P)
                            for x, w in ((xh, WH), (xl, WH), (xh, WL)):
                                last = nc.tensor.matmul(bank[:, 0:256], x[:, kt, rows_], w[:, s, cols],
                                                        start=kt == 0 and x is xh and w is WH, stop=kt == KT - 1 and w is WL)
                    last.then_inc(halves_done, 1)

            def norm_sum(parts, t):
                for part in parts:
                    bank = s_bank()
                    for i, k in enumerate(part):
                        if k % 2 == 0 or i == 0:
                            pe.wait_ge(sq_ready, n.next(sq_ready))
                        last = nc.tensor.matmul(bank[:, 0:t.stop - t.start], ones[:, 0:P], SQ[:, k, t],
                                                start=i == 0, stop=i == len(part) - 1)
                    last.then_inc(s_ready, 1)

            def transposes(src, count):
                bank = d_bank()
                for i in range(count):
                    last = nc.tensor.transpose(bank[:, i * P:(i + 1) * P], src[:, i * P:(i + 1) * P], ident)
                last.then_inc(d_ready, 1)

            def attention(units, score, values, pt):
                first_qb, last = units[0][1], len(units) - 1
                pe.wait_ge(d_free, n.at(d_ready))
                state = {}

                def turn(i):
                    pe.wait_ge(probn_ready, n.next(probn_ready))
                    for k in range(units[i][2] // P):
                        last_t = nc.tensor.transpose(DB[i % 2][:, k * P:(k + 1) * P], PR[:, i % 2, k * P:(k + 1) * P], ident)
                    last_t.then_inc(turned, 1)

                def weigh(i):
                    h, qb, nk = units[i]
                    if h % 2 == 0 and qb == first_qb:
                        state["bank"] = g_bank()
                    pe.wait_ge(pt_ready, n.next(pt_ready))
                    cols = slice((qb - first_qb) * P, (qb - first_qb + 1) * P)
                    b = VD * (h % 2)
                    product(state["bank"][b:b + VD, cols], [(values(k, h), pt[:, i % 2, k * P:(k + 1) * P]) for k in range(nk // P)]
                            ).then_inc(pv_done, 1)

                for i in range(-2, len(units)):
                    if i + 2 <= last:
                        score(s_bank(), *units[i + 2]).then_inc(s_ready, 1)
                    if 0 <= i + 1 <= last:
                        turn(i + 1)
                    if i >= 0:
                        weigh(i)

            def mod(l):
                p0 = PLAN["mod", l]
                pe.wait_ge(cl_ready, l + 1)
                for c in range(6):
                    bank = g_bank()
                    for i in range(4):
                        k = 2 * p0 + 4 * c + i
                        pe.wait_ge(lo_ready, k + 1)
                        for j in range(2):
                            kt = 2 * i + j
                            for x, w in ((XH, WH), (XL, WH), (XH, WL)):
                                last = nc.tensor.matmul(bank[:, :], x[:, kt // 4, kt % 4 * P:(kt % 4 + 1) * P],
                                                        w[:, k % SLOTS, j * 512:(j + 1) * 512],
                                                        start=kt == 0 and x is XH and w is WH, stop=kt == KT - 1 and w is WL)
                        last.then_inc(halves_done, 1)
                bank = g_bank()
                pe.wait_ge(modrow_ready, l + 1)
                for m in range(3 * KT):
                    last = nc.tensor.transpose(bank[:, 2 * m:2 * m + 2], MROW[0:2, m * P:(m + 1) * P], ident[0:2, 0:2])
                last.then_inc(g_ready, 1)

            def first_block(l):
                t = AT_ if l == 0 else XT
                mod(l)
                norm_sum([range(KT)], AT_)
                pe.wait_ge(xn_ready, n.next(xn_ready))
                p0 = PLAN["win", l]
                columns(2 * p0, 8, XH, XL, AT_)
                columns(2 * p0 + 8, 16, XH, XL, t)
                for i in range(2):
                    token_rows(2 * (PLAN["gv", l] + i), XH, XL, range(4))

                norm_sum([[0], [2, 3]], AT_)
                pe.wait_ge(lat_ready, n.next(lat_ready))
                pe.wait_ge(small_in, 16 * (l + 1))
                for h in range(HEADS):
                    product(d_bank()[0:QKD, 0:t.stop - t.start],
                            [(SW[:, SW_UQ + k * 768 + h * QKD:SW_UQ + k * 768 + (h + 1) * QKD], Z[:, Z_QLAT + k, t])
                             for k in range(2)]).then_inc(d_ready, 1)
                for h in range(HEADS):
                    product(d_bank()[0:NOPE, :], [(SW[:, SW_UK + h * NOPE:SW_UK + (h + 1) * NOPE], Z[:, Z_KV, :])]
                            ).then_inc(d_ready, 1)
                for tb in range(4):
                    product(d_bank()[:, :], [(Z[:, Z_KV, tb * P:(tb + 1) * P], SW[:, SW_UV:SW_UV + 512])]
                            ).then_inc(d_ready, 1)
                rot = C[KR:KR + ROPE, C_ROT:C_ROT + ROPE]
                product(d_bank()[KR:KR + ROPE, 0:SEQ], [(rot, Z[KR:KR + ROPE, Z_MISC, XT])]).then_inc(d_ready, 1)
                pe.wait_ge(qcopy_ready, n.next(qcopy_ready))
                for h in range(0, HEADS, 2):
                    product(d_bank()[KR:KR + ROPE, :].rearrange("p (h t) -> p h t", h=2),
                            [(rot, QB[KR:KR + ROPE, h:h + 2, XT])]).then_inc(d_ready, 1)
                pe.wait_ge(qkv_ready, n.next(qkv_ready))
                pe.wait_ge(kr_copied, n.next(kr_copied))
                attention(mla_units(l),
                          lambda bank, h, qb, nk: product(bank[:, 0:nk], [(QB[0:QKD, h, qb * P:(qb + 1) * P], KB[0:QKD, h, 0:nk])]),
                          lambda k, h: VM[:, k, h * VD:(h + 1) * VD], Z[:, Z_QLAT:Z_QLAT + 2, :])
                pe.wait_ge(pooled_ready, n.next(pooled_ready))
                for g in range(4):
                    product(d_bank()[:, 0:t.stop - t.start], [(SW[:, SW_PW + g * P:SW_PW + (g + 1) * P], PB[:, g, t])]
                            ).then_inc(d_ready, 1)
                for d, row in ((0, AF), (1, AB)):
                    for j in range(2):
                        product(d_bank()[:, :], [(SW[row:row + 16, SW_DW + j * P:SW_DW + (j + 1) * P], Z[row:row + 16, Z_MISC, :])]
                                ).then_inc(d_ready, 1)
                for d in range(2):
                    pe.wait_ge(decayed, n.next(decayed))
                    for j in range(2):
                        transposes(KDB[:, 2 * d + j, :], NCH)
                pe.wait_ge(kdt_ready, n.next(kdt_ready))
                for step in range(3):
                    bank = d_bank()
                    for d in range(2):
                        c = order[d][step]
                        for j in range(2):
                            for e in range(2):
                                h = 2 * j + e
                                col = (2 * d + j) * P
                                last = nc.tensor.matmul(bank[e * GDK:(e + 1) * GDK, col:col + GDV],
                                                        KDT[:, (2 * d + j) * NCH + c, e * GDK:(e + 1) * GDK],
                                                        VG[:, c, h * GDV:(h + 1) * GDV], start=True, stop=True)
                    last.then_inc(d_ready, 1)
                pe.wait_ge(state_ready, n.next(state_ready))
                first = 0 if l == 0 else 2
                for j in range(2):
                    banks = [g_bank(), g_bank()]
                    for c in range(first, NCH):
                        cc = slice(c * GCH, (c + 1) * GCH)
                        for e in range(2):
                            r = slice(e * GDK, (e + 1) * GDK)
                            bank = d_bank()
                            for d in range(2):
                                last = nc.tensor.matmul(bank[:, d * P:(d + 1) * P], KTB[r, 2 * d + j, cc],
                                                        QTB[r, 2 * d + j, cc], start=True, stop=True)
                            last.then_inc(d_ready, 1)
                        pe.wait_ge(gatt_ready, n.next(gatt_ready, 2))
                        for e in range(2):
                            r = slice(e * GDK, (e + 1) * GDK)
                            h = 2 * j + e
                            pairs = [(VG[:, c, h * GDV:(h + 1) * GDV], gatt(n.at(gatt_ready) // 2)[:, 2 * e + d, :]) for d in range(2)]
                            for d in range(2):
                                step = order[d].index(c) - 1
                                if step >= 0:
                                    pairs.append((ST[step][r, (2 * d + j) * P:(2 * d + j + 1) * P], QEB[r, 2 * d + j, cc]))
                            last = product(banks[e][:, (c - first) * GCH:(c - first + 1) * GCH], pairs)
                        last.then_inc(g_ready, 1)
                norm_sum([[0], [1], [2], [3]], t)
                pe.wait_ge(xn_ready, n.next(xn_ready))
                k0 = 2 * PLAN["merge", l]
                for b in range(3):
                    columns(k0 + 12 * b, 8, XH, XL, t)
                    pe.wait_ge(y_ready, n.next(y_ready))
                    columns(k0 + 12 * b + 8, 4, YH, YL, t, per_half=2, kts=4)
                pe.wait_ge(xn_ready, n.next(xn_ready))
                columns(2 * PLAN["wout", l], 8, XH, XL, t)
                norm_sum([range(KT)], t)

            def pre_norm():
                norm_sum([range(KT)], XT)
                pe.wait_ge(xn_ready, n.next(xn_ready))

            def ffn(i):
                pre_norm()
                p0 = PLAN[f"gate_up{i}"]
                columns(2 * p0, 2 * FB, XH, XL, XT)
                pe.wait_ge(g_free, blocks.at(g_free))
                pe.wait_ge(s_free, n.at(s_ready))
                pe.wait_ge(d_free, n.at(d_ready))
                banks = [g_bank() for _ in range(4)] + [*S, *DB]
                pe.wait_ge(hl_ready, FB * (i + 1))
                for u in range(FB):
                    k = 2 * PLAN[f"down{i}"] + u
                    pe.wait_ge(lo_ready, k + 1)
                    for m in range(KT):
                        for w, h in ((WH, HH), (WH, HL), (WL, HH)):
                            last = nc.tensor.matmul(banks[m][:, 0:SEQ], w[:, k % SLOTS, m * P:(m + 1) * P], h[:, u, :],
                                                    start=u == 0 and w is WH and h is HH, stop=u == FB - 1 and w is WL)
                    last.then_inc(halves_done, 1)
                pe.wait_ge(block_ready, n.next(block_ready))
                norm_sum([range(KT)], XT)

            pe.wait_ge(const_in, 32)
            for l in range(DEPTH):
                first_block(l)
            pre_norm()
            columns(2 * PLAN["attn_qk"], 16, XH, XL, XT)
            for i in range(4):
                token_rows(2 * (PLAN["attn_v"] + i), XH, XL, (2, 3))
            for kind, base, values in (("rel", 0, VA), ("stick", 8, VS)):
                pe.wait_ge(z_ready, n.next(z_ready))

                def score(bank, h, qb, nk, base=base):
                    r = slice(64 * (h % 2), 64 * (h % 2) + 64)
                    return product(bank[:, 0:nk], [(Z2[r, base + h // 2, qb * P:(qb + 1) * P], Z2[r, base + 4 + h // 2, :])])

                attention(b2_units, score, lambda k, h, values=values: values[:, k, h * VD:(h + 1) * VD], PT2)
            pe.wait_ge(xn_ready, n.next(xn_ready))
            columns(2 * PLAN["attn_out"], 8, XH, XL, XT)
            norm_sum([range(KT)], XT)
            ffn(0)
            pre_norm()
            columns(2 * PLAN["rg_in"], 16, XH, XL, XT)
            pe.wait_ge(xn_ready, n.next(xn_ready))
            columns(2 * PLAN["rg_ai"], 4, XH, XL, XT, per_half=4, kts=2, kt_of=lambda b, k: 2 * (b % 8 // 2) + k)
            pe.wait_ge(xn_ready, n.next(xn_ready))
            columns(2 * PLAN["rg_out"], 8, XH, XL, XT)
            norm_sum([range(KT)], XT)
            ffn(1)

        @block.scalar
        def _(act):
            n = Count()
            blocks = Count()
            A = nc.scalar.activation

            def link(ins):
                ins.then_inc(act_step, 1)
                act.wait_ge(act_step, n.next(act_step))

            def s_bank():
                b = n.next(s_ready)
                act.wait_ge(s_ready, b)
                return S[(b - 1) % 2]

            def halves(k):
                act.wait_ge(halves_done, k)

            def rstd(width, t, out):
                bank = s_bank()
                w = t.stop - t.start
                A(out[:, 0:w], bank[:, 0:w], ACT.Ln, bias=EPS, scale=1.0 / width).then_inc(s_free, 1)
                act.wait_ge(s_free, n.next(s_free))
                A(out[:, 0:w], out[:, 0:w], ACT.Exp, scale=-0.5).then_inc(rstd_ready, 1)

            def square(src, t):
                for k in range(0, KT, 2):
                    A(SQ[:, k:k + 2, t], src[:, k:k + 2, t], ACT.Square).then_inc(sq_ready, 1)

            def hi(k, g=None):
                if k >= HALVES:
                    return
                def at(x, m=TURN):
                    return x if g is None else g * m + x
                act.wait_ge(raw_in[k % SLOTS], at(16 * (k // SLOTS + 1), 16 * TURN // SLOTS))
                if k >= SLOTS:
                    act.wait_ge(halves_done, at(k - SLOTS + 1))
                A(WH[:, k % SLOTS, :], RAW[:, k % SLOTS, :], ACT.Copy).then_inc(hi_ready, 1)

            def steps(k0, count, evacuate=None):
                def body(i, g):
                    hi(k0 + i + SLOTS, g)
                    if evacuate:
                        act.wait_ge(halves_done, k0 + i + 1 if g is None else g * TURN + (k0 + i + 1))
                        evacuate(i, g)
                if count >= TURN:
                    with act.Fori(0, count // TURN) as g:
                        for i in range(TURN):
                            body(i, g)
                for i in range(count // TURN * TURN, count):
                    body(i, None)

            def copies(k0, count, buf, src_w, dst, off=0):
                base = blocks.at(g_free)

                def evacuate(i, g):
                    o = buf[:, i + off, dst] if g is None else (
                        buf[:, bass.ds(g * TURN + (i + off), 1), dst].rearrange("p a t -> p (a t)"))
                    A(o, G[(base + i) % 4][:, 0:src_w], ACT.Copy).then_inc(g_free, 1)
                steps(k0, count, evacuate)
                blocks.next(g_free, count)

            def upper(dst, src, t, pairs=4, st=None):
                for p in range(pairs):
                    act.wait_ge(xraw_ready, n.next(xraw_ready))
                    A(dst[:, 2 * p:2 * p + 2, t], src[:, 2 * p:2 * p + 2, st or t], ACT.Copy).then_inc(xh_ready, 1)

            def g_next():
                return G[(blocks.next(g_free) - 1) % 4]

            def keys_on_partitions(i, nk, pt):
                act.wait_ge(turned, n.next(turned))
                if i >= 2:
                    act.wait_ge(pv_done, n.at(pv_done) - 1)
                A(pt[:, i % 2, 0:nk], DB[i % 2][:, 0:nk], ACT.Copy).then_inc(pt_ready, 1)
                n.next(pv_done)

            def softmax_units(units, source, pt):
                def exponentials(i):
                    nk = units[i][2]
                    b = n.next(s_ready)
                    n.next(s_free)
                    if source is None:
                        act.wait_ge(s_ready, b)
                        src = S[(b - 1) % 2][:, 0:nk]
                    else:
                        src = source(i)[:, 0:nk]
                    act.wait_ge(rowmax_ready, n.next(rowmax_ready))
                    A(PR[:, i % 2, 0:nk], src, ACT.Exp, bias=STAT[:, i % 2, 0:1],
                      accum_out=STAT[:, i % 2, 1:2]).then_inc(prob_ready, 1)

                for i in range(-1, len(units)):
                    if i + 1 < len(units):
                        exponentials(i + 1)
                    if i >= 0:
                        keys_on_partitions(i, units[i][2], pt)

            EPS = V[:, NVEC - 1:NVEC]
            act.wait_ge(const_in, 32)
            for k in range(SLOTS):
                hi(k)
            cv = V[:, VEC["c"]:VEC["c"] + 2 * KT]
            link(A(cv, cv, ACT.Silu))
            lam = V[:, VEC["lam"]:VEC["lam"] + KT]
            link(A(LT[:, 0, :], lam, ACT.Abs))
            link(A(LT[:, 0, :], LT[:, 0, :], ACT.Exp, scale=-1.0))
            A(LT[:, 0, :], LT[:, 0, :], ACT.Ln, bias=1.0).then_inc(soft_ready, 1)
            act.wait_ge(x_in, 16)

            def first_block(l):
                t = AT_ if l == 0 else XT
                blocks.next(g_free, 7)
                if l > 0:
                    act.wait_ge(layer_done, n.next(layer_done))
                A(c_rep(XH), c_pairs(), ACT.Copy).then_inc(silu_c_ready, 1)
                square(X, AT_)
                steps(2 * PLAN["mod", l], 24)
                rstd(D, AT_, RA)
                upper(XH, XN, AT_)
                p0 = PLAN["win", l]
                copies(2 * p0, 12, Z, TOK, AT_) if l == 0 else (copies(2 * p0, 8, Z, TOK, AT_), copies(2 * p0 + 8, 4, Z, SEQ, XT, 8))
                copies(2 * p0 + 12, 12, ZG, t.stop - t.start, t)
                act.wait_ge(g_free, blocks.at(g_free))
                steps(2 * PLAN["gv", l], 4)
                blocks.next(g_free, 8)
                A(SQ[:, 0, :], Z[:, Z_KV, :], ACT.Square).then_inc(sq_ready, 1)
                A(SQ[:, 2:4, :], Z[:, Z_QLAT:Z_QLAT + 2, :], ACT.Square).then_inc(sq_ready, 1)
                A(ZG[:, :, t], ZG[:, :, t], ACT.Silu).then_inc(gates_ready, 1)
                rstd(KVR, AT_, RA)
                rstd(QR, AT_, PR[:, 0, :])
                act.wait_ge(kr_ready, n.next(kr_ready))
                A(KB[KR:KR + ROPE, :, :], Z[KR:KR + ROPE, Z_MISC, :].unsqueeze(1).to_broadcast([ROPE, HEADS, TOK]),
                  ACT.Copy).then_inc(kr_copied, 1)
                softmax_units(mla_units(l), None, Z[:, Z_QLAT:Z_QLAT + 2, :])
                blocks.next(g_free, 4)
                act.wait_ge(logit_ready, n.next(logit_ready))
                link(A(EX, LG, ACT.Abs))
                link(A(EX, EX, ACT.Exp, scale=-1.0))
                A(EX, EX, ACT.Ln, bias=1.0).then_inc(soft_ready, 1)
                for d in range(2):
                    r = slice(2 * d, 2 * d + 2)
                    act.wait_ge(expo_ready, n.next(expo_ready))
                    A(EE[:, 0:2, :], EX[:, 0:2, :], ACT.Exp, scale=1.0 / 16).then_inc(exp_ready, 1)
                    A(EE[:, 2:4, :], EX[:, 0:2, :], ACT.Exp, scale=-1.0 / 16).then_inc(exp_ready, 1)
                    act.wait_ge(expo_ready, n.next(expo_ready))
                    A(EE[:, 0:2, :], EX[:, 2:4, :], ACT.Exp, scale=1.0 / 16).then_inc(exp_ready, 1)
                    A(LG[:, r, :], LG[:, r, :], ACT.Exp, scale=1.0 / 16).then_inc(exp_ready, 1)
                blocks.next(g_free, 4)
                act.wait_ge(og_ready, n.next(og_ready))
                for h in range(GH):
                    A(SQ[:, h, t], OG[:, h, t], ACT.Square).then_inc(sq_ready, 1)
                upper(XH, XN, t)
                for h in range(GH):
                    w = t.stop - t.start
                    bank = s_bank()
                    A(SQ[:, 4 + h, t], bank[:, 0:w], ACT.Ln, bias=EPS, scale=1.0 / GDV).then_inc(s_free, 1)
                act.wait_ge(s_free, n.next(s_free, GH))
                A(SQ[:, 4:8, t], SQ[:, 4:8, t], ACT.Exp, scale=-0.5).then_inc(rstd_ready, 1)
                act.wait_ge(gla_done, n.next(gla_done))
                k0 = 2 * PLAN["merge", l]
                for b in range(3):
                    if b > 0:
                        act.wait_ge(merged_ready, n.next(merged_ready))
                    upper(YH, ZG[:, 4 * b:4 * b + 4, :], t, 2)
                    base = blocks.at(g_free)

                    def sigmoid(i, g):
                        A(SG[:, i, t], G[(base + i) % 4][:, 0:t.stop - t.start], ACT.Sigmoid).then_inc(g_free, 1)
                    steps(k0 + 12 * b, 8, sigmoid)
                    steps(k0 + 12 * b + 8, 4)
                    blocks.next(g_free, 16)
                n.next(merged_ready)
                upper(XH, MG, t)
                copies(2 * PLAN["wout", l], 8, XN, t.stop - t.start, t)
                act.wait_ge(g_free, blocks.at(g_free))
                square(XN, t)
                rstd(D, t, RA)

            def pre_norm():
                act.wait_ge(layer_done, n.next(layer_done))
                square(X, XT)
                rstd(D, XT, RA)
                upper(XH, XN, XT)

            def post_norm(wait=True):
                if wait:
                    act.wait_ge(g_free, blocks.at(g_free))
                square(XN, XT)
                rstd(D, XT, RA)

            def ffn(i):
                pre_norm()
                p0 = PLAN[f"gate_up{i}"]
                base = blocks.at(g_free)
                def silu(h, g):
                    if h % 2 == 0:
                        act.wait_ge(g_free, base + h - 2 if g is None else g * TURN + (base + h - 2))
                        A(PR[:, h // 2 % 2, 0:SEQ], G[(base + h) % 4][:, 0:SEQ], ACT.Silu).then_inc(silu_ready, 1)
                steps(2 * p0, 2 * FB, silu)
                blocks.next(g_free, 44 + 4)
                steps(2 * PLAN[f"down{i}"], FB)
                act.wait_ge(block_ready, n.next(block_ready))
                post_norm(False)

            for l in range(DEPTH):
                first_block(l)
            pre_norm()
            copies(2 * PLAN["attn_qk"], 16, Z2, SEQ, slice(0, SEQ))
            steps(2 * PLAN["attn_v"], 8)
            blocks.next(g_free, 8)
            softmax_units(b2_units, lambda i: SQ[:, i % 2, :], PT2)
            blocks.next(g_free, 4)

            def soft_part(i):
                bank = s_bank()
                n.next(s_free)
                T = SQ[:, i % 2, 0:SEQ]
                if i >= 2:
                    act.wait_ge(rowmax_ready, n.at(rowmax_ready) + i - 1)
                link(A(T, bank[:, 0:SEQ], ACT.Abs))
                link(A(T, T, ACT.Exp, scale=-1.0))
                A(T, T, ACT.Ln, bias=1.0).then_inc(soft_ready, 1)

            def weight_part(i):
                act.wait_ge(rowmax_ready, n.at(rowmax_ready) + i + 1)
                A(PR[:, i % 2, 0:SEQ], SQ[:, 4 + i % 2, 0:SEQ], ACT.Exp).then_inc(probn_ready, 1)

            for i in range(-2, len(b2_units)):
                if i + 2 < len(b2_units):
                    soft_part(i + 2)
                if 0 <= i + 1 < len(b2_units):
                    weight_part(i + 1)
                if i >= 0:
                    keys_on_partitions(i, SEQ, PT2)
            n.next(rowmax_ready, len(b2_units))
            blocks.next(g_free, 4)
            upper(XH, YB, XT, st=slice(0, SEQ))
            copies(2 * PLAN["attn_out"], 8, XN, SEQ, XT)
            post_norm()
            ffn(0)
            pre_norm()
            copies(2 * PLAN["rg_in"], 16, Z3, SEQ, slice(0, SEQ))
            act.wait_ge(g_free, blocks.at(g_free))
            A(Z3[:, 0:8, :], Z3[:, 0:8, :], ACT.Gelu_apprx_tanh).then_inc(gates_ready, 1)
            n.next(z_ready)
            p0 = PLAN["rg_ai"]
            upper(XH, XN, XT)
            for i, (dst, b) in enumerate(((QR_, "ba"), (KR_, "bi"))):
                for half in range(2):
                    k = 2 * (p0 + i) + half
                    hi(k + SLOTS)
                    act.wait_ge(halves_done, k)
                    for m in range(4 * half, 4 * half + 4):
                        if m % 4 == 0:
                            act.wait_ge(halves_done, k + 1)
                        A(dst[:, m, XT], g_next()[:, 0:SEQ], ACT.Sigmoid, bias=vec(b, m)).then_inc(g_free, 1)
            act.wait_ge(log_a_ready, 1)
            A(QR_[:, :, XT], QR_[:, :, CT], ACT.Exp).then_inc(exp_ready, 1)
            A(SQ[:, :, CT], QR_[:, :, CT], ACT.Tanh, scale=-1.0).then_inc(exp_ready, 1)
            A(SQ[:, :, XT], QR_[:, :, CT], ACT.Exp, scale=2.0).then_inc(exp_ready, 1)
            act.wait_ge(log_a_ready, 2)
            A(SQ[:, :, CT], SQ[:, :, CT], ACT.Sqrt).then_inc(exp_ready, 1)
            upper(XH, KR_, XT, st=CT)
            copies(2 * PLAN["rg_out"], 8, XN, SEQ, XT)
            post_norm()
            ffn(1)

        @block.vector
        def _(dve):
            n = Count()
            blocks = Count()
            v = nc.vector

            def link(ins):
                ins.then_inc(dve_step, 1)
                dve.wait_ge(dve_step, n.next(dve_step))

            def d_bank():
                b = n.next(d_ready)
                dve.wait_ge(d_ready, b)
                return DB[(b - 1) % 2]

            def s_bank():
                b = n.next(s_ready)
                dve.wait_ge(s_ready, b)
                return S[(b - 1) % 2]

            def g_next():
                return G[(blocks.next(g_free) - 1) % 4]

            def wait(s, k=1):
                dve.wait_ge(s, n.next(s, k))

            def skip_s(k=1):
                n.next(s_ready, k)
                n.next(s_free, k)

            def segs(l):
                return (CT, XT) if l == 0 else (XT,)

            def lo(k, g=None):
                if k < HALVES:
                    s = k % SLOTS
                    dve.wait_ge(hi_ready, k + 1 if g is None else g * TURN + (k + 1))
                    v.tensor_tensor(WL[:, s, :], RAW[:, s, :], WH[:, s, :].bitcast(f32), ALU.subtract).then_inc(lo_ready, 1)

            def steps(k0, count, evacuate=None):
                def body(i, g):
                    lo(k0 + i + SLOTS, g)
                    if evacuate:
                        evacuate(i, g)
                if count >= TURN:
                    with dve.Fori(0, count // TURN) as g:
                        for i in range(TURN):
                            body(i, g)
                for i in range(count // TURN * TURN, count):
                    body(i, None)

            def lower(dh, dl, src, t, pairs=4, st=None, done=None, announce=False):
                if announce:
                    dve.sem_inc(xraw_ready, pairs)
                for p in range(pairs):
                    wait(xh_ready)
                    r = slice(2 * p, 2 * p + 2)
                    last = v.tensor_tensor(dl[:, r, t], src[:, r, st or t], dh[:, r, t].bitcast(f32), ALU.subtract)
                last.then_inc(done or xn_ready, 1)

            def gv_copies(k0, dsts, tbs, off=0):
                dve.wait_ge(g_free, blocks.at(g_free))
                for i, (dst, col) in enumerate(dsts):
                    k = k0 + 2 * i
                    lo(k + SLOTS)
                    lo(k + 1 + SLOTS)
                    dve.wait_ge(halves_done, k + 2)
                    for tb in tbs:
                        v.tensor_copy(dst[:, tb, col:col + 256], g_next()[:, 0:256]).then_inc(g_free, 1)

            def add_normed(t_segs, gain):
                wait(rstd_ready)
                skip_s()
                off = t_segs[0].start
                for t in t_segs:
                    for k in range(KT):
                        r = RA[:, t.start - off:t.stop - off]
                        last = v.scalar_tensor_tensor(out=XN[:, k, t], in0=XN[:, k, t], scalar=gain(k, t), in1=r,
                                                      op0=ALU.mult, op1=ALU.mult)
                link(last)
                for t in t_segs:
                    last = v.tensor_tensor(X[:, :, t], X[:, :, t], XN[:, :, t], ALU.add)
                last.then_inc(layer_done, 1)
                dve.wait_ge(layer_done, n.next(layer_done))

            def plain_norm(gain):
                wait(rstd_ready)
                skip_s()
                for k in range(KT):
                    last = v.scalar_tensor_tensor(out=XN[:, k, XT], in0=X[:, k, XT], scalar=gain(k), in1=RA[:, 0:SEQ],
                                                  op0=ALU.mult, op1=ALU.mult)
                    if k % 2:
                        last.then_inc(xraw_ready, 1)
                lower(XH, XL, XN, XT)

            def out_of_bank(units, i, out):
                first_qb, last_qb = units[0][1], units[-1][1]
                if i >= 0:
                    n.next(pv_done)
                    h, qb, _ = units[i]
                    if h % 2 == 1 and qb == last_qb:
                        dve.wait_ge(pv_done, n.at(pv_done))
                        out(h // 2, g_next()[:, 0:(last_qb - first_qb + 1) * P])

            def softmax_units(units, rel, out):
                def front(i):
                    h, qb, nk = units[i]
                    bank = s_bank()
                    n.next(s_free)
                    if rel:
                        s = SQ[:, i % 2, 0:nk]
                        v.tensor_tensor(s, bank[:, 0:nk], BT[:, 2 * h + qb, :], ALU.add).then_inc(s_free, 1)
                        dve.wait_ge(s_free, n.at(s_free))
                    else:
                        s = bank[:, 0:nk]
                    v.tensor_reduce(STAT[:, i % 2, 0:1], s, AX, ALU.max, negate=True).then_inc(rowmax_ready, 1)

                def back(i):
                    st, p = STAT[:, i % 2, :], PR[:, i % 2, 0:units[i][2]]
                    wait(prob_ready)
                    if rel:
                        link(v.reciprocal(st[:, 2:3], st[:, 1:2]))
                    else:
                        v.reciprocal(st[:, 2:3], st[:, 1:2]).then_inc(s_free, 1)
                        dve.wait_ge(s_free, n.at(s_free) - (1 if i + 1 < len(units) else 0))
                    v.tensor_scalar(p, p, st[:, 2:3], None, ALU.mult).then_inc(probn_ready, 1)
                    n.next(probn_ready)

                for i in range(-1, len(units)):
                    if i + 1 < len(units):
                        front(i + 1)
                    if i >= 0:
                        back(i)
                        out_of_bank(units, i - 2, out)
                for i in (len(units) - 2, len(units) - 1):
                    out_of_bank(units, i, out)

            dve.wait_ge(const_in, 32)
            for k in range(SLOTS):
                lo(k)
            wait(soft_ready)
            lam = V[:, VEC["lam"]:VEC["lam"] + KT]
            link(v.tensor_scalar(LT[:, 1, :], lam, -1.0, 0.0, ALU.mult, ALU.max))
            link(v.tensor_tensor(LT[:, 1, :], LT[:, 1, :], LT[:, 0, :], ALU.add))
            link(v.tensor_scalar(NLAM[:, :], LT[:, 1, :], -8.0, None, ALU.mult))

            def first_block(l):
                t = AT_ if l == 0 else XT
                w = t.stop - t.start
                p0 = PLAN["mod", l]
                dve.wait_ge(silu_c_ready, l + 1)
                v.tensor_tensor(c_rep(XL), c_pairs(), c_rep(XH).bitcast(f32), ALU.subtract).then_inc(cl_ready, 1)
                for c in range(6):
                    for i in range(4):
                        lo(2 * p0 + 4 * c + i + SLOTS)
                    dve.wait_ge(halves_done, 2 * p0 + 4 * c + 4)
                    v.tensor_copy(MROW[0:2, c * 512:(c + 1) * 512], g_next()[0:2, :]).then_inc(g_free, 1)
                dve.wait_ge(g_free, blocks.at(g_free))
                dve.sem_inc(modrow_ready, 1)
                wait(g_ready)
                b0 = VEC["mod_b"] + l * 6 * KT
                v.tensor_tensor(MOD[:, :, :], g_next()[:, 0:6 * KT].rearrange("p (a b) -> p a b", b=2),
                                V[:, b0:b0 + 6 * KT].rearrange("p (a b) -> p a b", b=2), ALU.add).then_inc(g_free, 1)
                dve.wait_ge(g_free, blocks.at(g_free))

                def both(name):
                    b = VEC[name] + l * KT
                    return V[:, b:b + KT].unsqueeze(2).to_broadcast([P, KT, 2])

                v.scalar_tensor_tensor(out=AMOD[:, :, :], in0=MOD[:, KT:2 * KT, :], scalar=1.0, in1=both("pre"),
                                       op0=ALU.add, op1=ALU.mult)
                link(v.tensor_tensor(GPOST[:, :, :], MOD[:, 2 * KT:, :], both("post"), ALU.mult))
                wait(rstd_ready)
                skip_s()
                for k in range(KT):
                    for s in (CT, XT):
                        e = seg(s)
                        last = v.scalar_tensor_tensor(out=XN[:, k, s], in0=X[:, k, s], scalar=AMOD[:, k, e:e + 1],
                                                      in1=RA[:, s], op0=ALU.mult, op1=ALU.mult)
                link(last)
                for k in range(KT):
                    for s in (CT, XT):
                        e = seg(s)
                        last = v.tensor_scalar(XN[:, k, s], XN[:, k, s], MOD[:, k, e:e + 1], None, ALU.add)
                    if k % 2:
                        last.then_inc(xraw_ready, 1)
                lower(XH, XL, XN, AT_)
                steps(2 * PLAN["win", l], 24)
                blocks.next(g_free, 24)
                gv_copies(2 * PLAN["gv", l], ((VG, 0), (VG, 256)), range(4))
                skip_s(2)
                wait(rstd_ready)
                v.scalar_tensor_tensor(out=Z[:, Z_KV, :], in0=Z[:, Z_KV, :], scalar=vec("kvn", l), in1=RA[:, :],
                                       op0=ALU.mult, op1=ALU.mult)
                wait(rstd_ready)
                for k in range(2):
                    last = v.scalar_tensor_tensor(out=Z[:, Z_QLAT + k, :], in0=Z[:, Z_QLAT + k, :],
                                                  scalar=vec("qn", 2 * l + k), in1=PR[:, 0, :], op0=ALU.mult, op1=ALU.mult)
                last.then_inc(lat_ready, 1)
                for h in range(HEADS):
                    v.tensor_scalar(QB[0:QKD, h, t], d_bank()[0:QKD, 0:w], float(QKD) ** -0.5, None, ALU.mult).then_inc(d_free, 1)
                dve.wait_ge(d_free, n.at(d_ready))
                dve.sem_inc(qcopy_ready, 1)
                for h in range(HEADS):
                    v.tensor_copy(KB[0:NOPE, h, :], d_bank()[0:NOPE, :]).then_inc(d_free, 1)
                for tb in range(4):
                    v.tensor_copy(VM[:, tb, :], d_bank()[:, :]).then_inc(d_free, 1)
                r = slice(KR, KR + ROPE)
                cos, sin = C[r, C_COS:C_COS + SEQ], C[r, C_SIN:C_SIN + SEQ]
                tmp = SQ[r, 4:6, 0:SEQ]
                v.tensor_tensor(tmp[:, 0, :], d_bank()[r, 0:SEQ], sin, ALU.mult).then_inc(d_free, 1)
                link(v.tensor_tensor(Z[r, Z_MISC, XT], Z[r, Z_MISC, XT], cos, ALU.mult))
                v.tensor_tensor(Z[r, Z_MISC, XT], Z[r, Z_MISC, XT], tmp[:, 0, :], ALU.add).then_inc(kr_ready, 1)
                dve.wait_ge(kr_ready, n.next(kr_ready))
                for h in range(0, HEADS, 2):
                    q = QB[r, h:h + 2, XT]
                    v.tensor_tensor(tmp, d_bank()[r, :].rearrange("p (h t) -> p h t", h=2),
                                    sin.unsqueeze(1).to_broadcast([ROPE, 2, SEQ]), ALU.mult).then_inc(d_free, 1)
                    link(v.tensor_tensor(q, q, cos.unsqueeze(1).to_broadcast([ROPE, 2, SEQ]), ALU.mult))
                    last = v.tensor_tensor(q, q, tmp, ALU.add)
                    if h < HEADS - 2:
                        link(last)
                last.then_inc(qkv_ready, 1)
                wait(gates_ready)

                def gated(j, o):
                    v.tensor_tensor(ZG[:, j, t], o, ZG[:, j, t], ALU.mult).then_inc(g_free, 1)

                softmax_units(mla_units(l), False, gated)
                for s in segs(l):
                    for g in range(4):
                        v.memset(CS[:, g, 0:PADW + 1], 0.0)
                        last = v.tensor_tensor_scan(CS[:, g, PADW + 1:PADW + 1 + SEQ], ones, Z[:, Z_POOL + g, s], 0.0,
                                                    ALU.mult, ALU.add)
                    link(last)
                    link(v.tensor_copy(CS[:, :, PADW + 1 + SEQ:], CS[:, :, PADW + SEQ:PADW + SEQ + 1]
                                       .to_broadcast([P, 4, PADW - 1])))
                    for g, win in enumerate(WINDOWS):
                        after, before = PADW + win // 2, PADW - win // 2
                        last = v.tensor_tensor(PB[:, g, s], CS[:, g, after:after + SEQ], CS[:, g, before:before + SEQ], ALU.subtract)
                    link(last)
                    edge = C[:, C_EDGE:C_EDGE + 8 * PADW].rearrange("p (g e t) -> p g e t", g=4, e=2)
                    for e, cols in enumerate((slice(s.start, s.start + PADW), slice(s.stop - PADW, s.stop))):
                        last = v.tensor_tensor(PB[:, :, cols], PB[:, :, cols], edge[:, :, e, :], ALU.mult)
                    link(last)
                    for g, win in enumerate(WINDOWS):
                        last = v.scalar_tensor_tensor(out=PB[:, g, s], in0=PB[:, g, s], scalar=1.0 / win,
                                                      in1=Z[:, Z_POOL + g, s], op0=ALU.mult, op1=ALU.subtract)
                    if s is not segs(l)[-1]:
                        link(last)
                last.then_inc(pooled_ready, 1)
                for g in range(4):
                    gate = ZG[:, 4 + g, t]
                    v.scalar_tensor_tensor(out=gate, in0=d_bank()[:, 0:w], scalar=vec("pscale", 4 * l + g), in1=gate,
                                           op0=ALU.mult, op1=ALU.mult).then_inc(d_free, 1)
                for i in range(4):
                    last = v.tensor_scalar(LG[:, i, :], d_bank()[:, :], vec("gab", 4 * l + i), None, ALU.add)
                    last.then_inc(d_free, 1)
                dve.wait_ge(d_free, n.at(d_ready))
                dve.sem_inc(logit_ready, 1)
                wait(soft_ready)
                link(v.scalar_tensor_tensor(out=EE, in0=LG, scalar=0.0, in1=EX, op0=ALU.min, op1=ALU.subtract))
                for d in range(2):
                    for j in range(2):
                        for c in range(NCH):
                            a = slice(c * GCH, (c + 1) * GCH) if d == 0 else (
                                slice((c + 1) * GCH - 1, c * GCH - 1 if c else None, -1))
                            last = v.tensor_tensor_scan(LG[:, 2 * d + j, a], ones[:, 0:GCH], EE[:, 2 * d + j, a], 0.0,
                                                        ALU.mult, ALU.add)
                link(last)
                for d in range(2):
                    r = slice(2 * d, 2 * d + 2)
                    mid, end = (GCH // 2 - 1, GCH - 1) if d == 0 else (GCH // 2, 0)
                    b = LG[:, r, :].rearrange("p j (c t) -> p (j c) t", t=GCH)
                    x0 = EX[:, 0:2, :].rearrange("p j (c t) -> p (j c) t", t=GCH)
                    x1 = EX[:, 2:4, :].rearrange("p j (c t) -> p (j c) t", t=GCH)
                    link(v.tensor_tensor(x0, b, b[:, :, mid:mid + 1].to_broadcast([P, 2 * NCH, GCH]), ALU.subtract))
                    v.tensor_scalar(EX[:, 0:2, :], EX[:, 0:2, :], -16 * CLAMP, 16 * CLAMP, ALU.max, ALU.min).then_inc(expo_ready, 1)
                    wait(exp_ready, 2)
                    q, k = Z[:, Z_GQ:Z_GQ + 2, :], Z[:, Z_GK:Z_GK + 2, :]
                    fl = lambda a: a.rearrange("p j t -> p (j t)")
                    v.scalar_tensor_tensor(out=QTB[:, r, :], in0=EE[:, 0:2, :], scalar=GDK ** -0.5, in1=q, op0=ALU.mult, op1=ALU.mult)
                    v.tensor_tensor(KTB[:, r, :], EE[:, 2:4, :], k, ALU.mult)
                    v.tensor_tensor(x1, b[:, :, end:end + 1].to_broadcast([P, 2 * NCH, GCH]), b, ALU.subtract).then_inc(expo_ready, 1)
                    wait(exp_ready, 2)
                    v.scalar_tensor_tensor(out=QEB[:, r, :], in0=LG[:, r, :], scalar=GDK ** -0.5, in1=q, op0=ALU.mult, op1=ALU.mult)
                    v.tensor_tensor(KDB[:, r, :], EE[:, 0:2, :], k, ALU.mult).then_inc(decayed, 1)
                    dve.wait_ge(decayed, n.next(decayed))
                for i in range(4):
                    v.tensor_copy(KDT[:, i * NCH:(i + 1) * NCH, :], d_bank()[:, :].rearrange("p (a b) -> p a b", b=P)).then_inc(d_free, 1)
                dve.wait_ge(d_free, n.at(d_ready))
                dve.sem_inc(kdt_ready, 1)
                for step in range(3):
                    bank = d_bank()
                    if step == 0:
                        last = v.tensor_copy(ST[0], bank[:, :])
                    else:
                        for d in range(2):
                            c = order[d][step]
                            end = c * GCH + (GCH - 1 if d == 0 else 0)
                            for j in range(2):
                                i = 2 * d + j
                                last = v.scalar_tensor_tensor(out=ST[step][:, i * P:(i + 1) * P], in0=ST[step - 1][:, i * P:(i + 1) * P],
                                                              scalar=LG[:, i, end:end + 1], in1=bank[:, i * P:(i + 1) * P],
                                                              op0=ALU.mult, op1=ALU.add)
                    last.then_inc(d_free, 1)
                    dve.wait_ge(d_free, n.at(d_ready))
                dve.sem_inc(state_ready, 1)
                first = 0 if l == 0 else 2
                mask = C[:, C_MASK:C_MASK + 256]
                for j in range(2):
                    for c in range(first, NCH):
                        i = n.next(gatt_ready, 2) // 2
                        for e in range(2):
                            bank = d_bank()
                            v.scalar_tensor_tensor(out=gatt(i)[:, 2 * e:2 * e + 2, :].rearrange("p a b -> p (a b)"),
                                                   in0=bank[:, 0:256], scalar=3.0e38, in1=mask,
                                                   op0=ALU.min, op1=ALU.mult).then_inc(gatt_ready, 1)
                            dve.wait_ge(gatt_ready, n.at(gatt_ready) - 1 + e)
                            dve.sem_inc(d_free, 1)
                    wait(g_ready, NCH - first)
                    for e in range(2):
                        last = v.tensor_copy(OG[:, 2 * j + e, t], g_next()[:, 0:w])
                        last.then_inc(g_free, 1)
                dve.wait_ge(g_free, blocks.at(g_free))
                dve.sem_inc(og_ready, 1)
                lower(XH, XL, XN, t, announce=True)
                skip_s(4)
                wait(rstd_ready)
                for h in range(GH):
                    last = v.scalar_tensor_tensor(out=OG[:, h, t], in0=OG[:, h, t], scalar=vec("gn", l), in1=SQ[:, 4 + h, t],
                                                  op0=ALU.mult, op1=ALU.mult)
                link(last)
                v.tensor_tensor(ZG[:, 8:, t], ZG[:, 8:, t], OG[:, :, t], ALU.mult).then_inc(gla_done, 1)
                dve.wait_ge(gla_done, n.next(gla_done))
                k0 = 2 * PLAN["merge", l]
                for b in range(3):
                    lower(YH, YL, ZG[:, 4 * b:4 * b + 4, :], t, 2, done=y_ready, announce=True)
                    blocks.next(g_free, 8)
                    steps(k0 + 12 * b, 8)
                    dve.wait_ge(g_free, blocks.at(g_free))
                    for half in range(4):
                        lo(k0 + 12 * b + 8 + half + SLOTS)
                        dve.wait_ge(halves_done, k0 + 12 * b + 8 + half + 1)
                        for i in (2 * half, 2 * half + 1):
                            v.tensor_tensor((SG if b else MG)[:, i, t], g_next()[:, 0:w], SG[:, i, t], ALU.mult).then_inc(g_free, 1)
                    dve.wait_ge(g_free, blocks.at(g_free))
                    m = n.next(merged_ready)
                    if b == 0:
                        dve.sem_inc(merged_ready, 1)
                    else:
                        v.tensor_tensor(MG[:, :, t], MG[:, :, t], SG[:, :, t], ALU.add).then_inc(merged_ready, 1)
                        dve.wait_ge(merged_ready, m)
                lower(XH, XL, MG, t, announce=True)
                steps(2 * PLAN["wout", l], 8)
                blocks.next(g_free, 8)
                add_normed(segs(l), lambda k, s: GPOST[:, k, seg(s):seg(s) + 1])

            def ffn(i):
                plain_norm(lambda k: vec("ffnpre", KT * i + k))
                p0 = PLAN[f"gate_up{i}"]
                base = blocks.at(g_free)
                def product(h, g):
                    f = h // 2
                    if h % 2 == 0:
                        return
                    def at(x, m=TURN // 2):
                        return x if g is None else g * m + x
                    dve.wait_ge(silu_ready, at(FB * i + f + 1))
                    dve.wait_ge(halves_done, at(2 * p0 + h + 1, TURN))
                    if i or g is not None or f >= 3:
                        dve.wait_ge(hl_ready, at(FB * i + f - 2))
                    v.tensor_tensor(XN[:, f % 3, XT], PR[:, f % 2, 0:SEQ], G[(base + h) % 4][:, 0:SEQ], ALU.mult).then_inc(hraw_ready, 1)
                    dve.wait_ge(hraw_ready, at(FB * i + f + 1))
                    dve.sem_inc(g_free, 2)
                if i == 0:
                    for h in range(TURN):
                        lo(2 * p0 + h + SLOTS)
                        product(h, None)
                    with dve.Fori(1, 2 * FB // TURN) as g:
                        for h in range(TURN):
                            lo(2 * p0 + h + SLOTS, g)
                            product(h, g)
                    for h in range(2 * FB // TURN * TURN, 2 * FB):
                        lo(2 * p0 + h + SLOTS)
                        product(h, None)
                else:
                    steps(2 * p0, 2 * FB, product)
                blocks.next(g_free, 2 * FB)
                steps(2 * PLAN[f"down{i}"], FB)
                dve.wait_ge(halves_done, 2 * (PLAN[f"down{i}"] + 11))
                dve.wait_ge(hl_ready, FB * (i + 1))
                banks = [g_next() for _ in range(4)] + [*S, *DB]
                for m in range(KT):
                    last = v.tensor_copy(XN[:, m, XT], banks[m][:, 0:SEQ])
                last.then_inc(g_free, 4)
                dve.wait_ge(g_free, blocks.at(g_free))
                dve.sem_inc(block_ready, 1)
                add_normed((XT,), lambda k, s: vec("ffnpost", KT * i + k))

            for l in range(DEPTH):
                first_block(l)
            dve.sem_inc(block1_free, 1)
            plain_norm(lambda k: vec("mixpre", k))
            steps(2 * PLAN["attn_qk"], 16)
            blocks.next(g_free, 16)
            gv_copies(2 * PLAN["attn_v"], ((VA, 0), (VA, 256), (VS, 0), (VS, 256)), (0, 1))
            dve.wait_ge(g_free, blocks.at(g_free))
            v.tensor_scalar(Z2[:, 0:4, :], Z2[:, 0:4, :], 0.125, None, ALU.mult).then_inc(z_ready, 1)
            dve.wait_ge(bias_in, 32)
            bt4 = BT[:, :, :].rearrange("p (h q) t -> p h q t", q=2)
            for qb in range(2):
                last = v.tensor_tensor(bt4[:, :, qb, :], bt4[:, :, qb, :],
                                       causal_neg[:, qb, :].unsqueeze(1).to_broadcast([P, HEADS, SEQ]), ALU.add)
            link(last)
            v.tensor_scalar(Z2[:, 8:12, :], Z2[:, 8:12, :], 0.125, None, ALU.mult).then_inc(z_ready, 1)

            def copied(off):
                def out(j, o):
                    v.tensor_copy(YB[:, off + j, :], o).then_inc(g_free, 1)
                return out

            softmax_units(b2_units, True, copied(0))

            def sticks(i):
                h, qb, nk = b2_units[i]
                bank = s_bank()
                T, R = SQ[:, i % 2, 0:SEQ], SQ[:, 2 + i % 2, 0:SEQ]
                W = SQ[:, 4 + i % 2, 0:SEQ]
                wait(soft_ready)
                link(v.scalar_tensor_tensor(out=T, in0=bank[:, 0:SEQ], scalar=0.0, in1=T, op0=ALU.max, op1=ALU.add))
                link(v.tensor_tensor(T, T, strict[:, qb, :], ALU.mult))
                link(v.tensor_tensor_scan(R[:, ::-1], ones, T[:, ::-1], 0.0, ALU.mult, ALU.add))
                v.tensor_tensor(R, bank[:, 0:SEQ], R, ALU.subtract).then_inc(s_free, 1)
                dve.wait_ge(s_free, n.next(s_free))
                if i >= 2:
                    dve.wait_ge(probn_ready, n.at(probn_ready) + i - 1)
                v.tensor_tensor(W, R, strict_neg[:, qb, :], ALU.add).then_inc(rowmax_ready, 1)

            for i in range(len(b2_units)):
                sticks(i)
                out_of_bank(b2_units, i - 3, copied(4))
            for i in range(len(b2_units) - 3, len(b2_units)):
                out_of_bank(b2_units, i, copied(4))
            dve.wait_ge(g_free, blocks.at(g_free))
            lower(XH, XL, YB, XT, st=slice(0, SEQ), announce=True)
            steps(2 * PLAN["attn_out"], 8)
            blocks.next(g_free, 8)
            add_normed((XT,), lambda k, s: vec("mixpost", k))
            ffn(0)
            plain_norm(lambda k: vec("mixpre", KT + k))
            steps(2 * PLAN["rg_in"], 16)
            blocks.next(g_free, 16)
            wait(gates_ready)
            for k in range(KT):
                last = v.tensor_scalar(XN[:, k, XT], Z3[:, 8 + k, :], vec("convw", 3 * KT + k), vec("convb", k), ALU.mult, ALU.add)
            for back in range(1, 4):
                link(last)
                for k in range(KT):
                    o = XN[:, k, CTX + back:TOK]
                    last = v.scalar_tensor_tensor(out=o, in0=Z3[:, 8 + k, 0:SEQ - back], scalar=vec("convw", (3 - back) * KT + k),
                                                  in1=o, op0=ALU.mult, op1=ALU.add)
            link(last)
            lower(XH, XL, XN, XT, announce=True)
            steps(2 * PLAN["rg_ai"], 4)
            blocks.next(g_free, 16)
            dve.wait_ge(g_free, blocks.at(g_free) - 8)
            for k in range(KT):
                last = v.tensor_scalar(QR_[:, k, CT], QR_[:, k, XT], NLAM[:, k:k + 1], None, ALU.mult)
            last.then_inc(log_a_ready, 1)
            wait(exp_ready, 3)
            v.scalar_tensor_tensor(out=SQ[:, :, CT], in0=SQ[:, :, XT], scalar=1.0, in1=SQ[:, :, CT],
                                   op0=ALU.add, op1=ALU.mult).then_inc(log_a_ready, 1)
            dve.wait_ge(g_free, blocks.at(g_free))
            link(v.tensor_tensor(KR_[:, :, XT], KR_[:, :, XT], XN[:, :, XT], ALU.mult))
            wait(exp_ready)
            link(v.tensor_tensor(KR_[:, :, XT], KR_[:, :, XT], SQ[:, :, CT], ALU.mult))
            for k in range(KT):
                last = v.tensor_tensor_scan(KR_[:, k, CT], QR_[:, k, XT], KR_[:, k, XT], 0.0, ALU.mult, ALU.add)
            link(last)
            link(v.tensor_tensor(KR_[:, :, CT], KR_[:, :, CT], Z3[:, 0:8, :], ALU.mult))
            lower(XH, XL, KR_, XT, st=CT, announce=True)
            steps(2 * PLAN["rg_out"], 8)
            blocks.next(g_free, 8)
            add_normed((XT,), lambda k, s: vec("mixpost", KT + k))
            ffn(1)


def constants():
    import numpy as np
    f = np.float32
    c = np.zeros((P, NCONST), f)
    c[:, C_ONES:C_ONES + 256] = 1
    c[:, C_ID:C_ID + P] = np.eye(P)
    key, query = np.arange(P)[:, None], np.arange(P)[None, :]
    c[:, C_MASK:C_MASK + P] = key <= query
    c[:, C_MASK + P:C_MASK + 2 * P] = key >= query
    inv = (f(10000.0) ** (-np.arange(0, ROPE // 2, 2, dtype=f) / f(ROPE // 2))).astype(f)
    t = np.arange(SEQ)
    ang = np.concatenate([(t // 64).astype(f)[None] * inv[:, None]] * 2 + [(t % 64).astype(f)[None] * inv[:, None]] * 2)
    c[KR:KR + ROPE, C_COS:C_COS + SEQ] = np.cos(ang)
    c[KR:KR + ROPE, C_SIN:C_SIN + SEQ] = np.sin(ang)
    for m in range(ROPE):
        c[KR + (m + 8 if m % 16 < 8 else m - 8), C_ROT + m] = -1 if m % 16 < 8 else 1
    for g, w in enumerate(WINDOWS):
        for e, ts in enumerate((np.arange(PADW), np.arange(SEQ - PADW, SEQ))):
            count = np.minimum(ts + w // 2, SEQ) - np.maximum(ts - w // 2, 0)
            at = C_EDGE + (2 * g + e) * PADW
            c[:, at:at + PADW] = w / count
    q = np.arange(SEQ).reshape(2, P).T[:, :, None]
    k = np.arange(SEQ)[None, None, :]
    c2 = np.concatenate([(k < q).astype(f), np.where(k < q, 0, -1e30).astype(f),
                         np.where(k // 64 <= q // 64, 0, -1e30).astype(f)], axis=1)
    return c, np.ascontiguousarray(c2)


def kernel(**inputs):
    import numpy as np
    import concourse.bacc as bacc
    from concourse.bass_utils import run_bass_kernel_spmd

    a = {n: np.asarray(x) for n, x in inputs.items()}
    ws = np.empty((HALVES, P, HALF), np.float32)

    def put(at, x):
        ws[2 * at:2 * (at + len(x))] = x.reshape(len(x), P, 2, HALF).transpose(0, 2, 1, 3).reshape(-1, P, HALF)

    def cols(w, per=2):
        k = w.shape[0] // P
        return w.reshape(k, P, -1, per, P).transpose(2, 1, 3, 0, 4)

    def rows(w):
        return w.reshape(KT, P, -1, 256).transpose(2, 1, 0, 3)

    ends = np.cumsum([0, QR, KVR, ROPE, 512, 512, 512, 256, 256, 512, 16, 16, 512, 3 * D])
    names = ("q", "kv", "kr", "mg", "px", "pg", "gq", "gk", "gv", "af", "ab", "gg", "merge")
    small = np.zeros((DEPTH, P, NSW), np.float32)
    for l in range(DEPTH):
        w = {n: a["w_in"][l][:, ends[i]:ends[i + 1]] for i, n in enumerate(names)}
        pad = np.zeros((D, 16), np.float32)
        win = np.concatenate([w["kv"], w["af"], pad, w["ab"], pad, w["kr"], pad, pad, w["gk"], w["gq"], w["q"],
                              w["px"], w["mg"], w["pg"], w["gg"]], axis=1)
        put(PLAN["mod", l], a["mod_w"][l].reshape(2, 4, P, 6, 512).transpose(3, 0, 2, 1, 4).reshape(12, P, -1))
        put(PLAN["win", l], cols(win))
        put(PLAN["gv", l], rows(w["gv"]))
        for b, branch in enumerate(("w_branch_mla", "w_branch_pool", "w_branch_gla")):
            put(PLAN["merge", l] + 6 * b, cols(w["merge"][:, b * D:(b + 1) * D]))
            put(PLAN["merge", l] + 6 * b + 4, cols(a[branch][l], 4))
        put(PLAN["wout", l], cols(a["w_out"][l]))
        small[l, :, SW_UQ:SW_UK] = a["mla_w_uq"][l].reshape(2, P, -1).transpose(1, 0, 2).reshape(P, -1)
        ukv = a["mla_w_ukv"][l].reshape(P, HEADS, NOPE + VD)
        small[l, :, SW_UK:SW_UV] = ukv[:, :, :NOPE].reshape(P, -1)
        small[l, :, SW_UV:SW_PW] = ukv[:, :, NOPE:].reshape(P, -1)
        small[l, :, SW_PW:SW_DW] = a["pool_w"][l].transpose(1, 0, 2).reshape(P, -1)
        small[l, AF:AF + 16, SW_DW:NSW] = a["gla_af_w2"][l]
        small[l, AB:AB + 16, SW_DW:NSW] = a["gla_ab_w2"][l]
    ain = a["attn_w_in_2"][0].reshape(D, 6, 512)
    put(PLAN["attn_qk"], cols(np.ascontiguousarray(ain[:, [0, 1, 3, 4]]).reshape(D, -1)))
    put(PLAN["attn_v"], rows(np.ascontiguousarray(ain[:, [2, 5]]).reshape(D, -1)))
    put(PLAN["attn_out"], cols(a["attn_w_out_2"][0]))
    put(PLAN["rg_in"], cols(a["rg_w_in_2"][0]))
    for i, n in enumerate(("rg_w_a_2", "rg_w_i_2")):
        put(PLAN["rg_ai"] + i, a[n][0].reshape(4, 2, P, 2, P).transpose(2, 0, 3, 1, 4)[None])
    put(PLAN["rg_out"], cols(a["rg_w_out_2"][0]))
    for i in range(2):
        gate, up = (cols(a[n][i], 1) for n in ("ffn_w_gate_2", "ffn_w_up_2"))
        put(PLAN[f"gate_up{i}"], np.concatenate([gate, up], axis=2))
        put(PLAN[f"down{i}"], a["ffn_w_down_2"][i].reshape(FB // 2, 2, P, KT, P).transpose(0, 2, 1, 3, 4))

    vecs = np.zeros((P, NVEC), np.float32)

    def column(name, x, at=0):
        x = x.reshape(-1, P).T
        vecs[:, VEC[name] + at:VEC[name] + at + x.shape[1]] = x

    both = np.stack([a["c_ctx"], a["c"][0]])
    vecs[:, VEC["c"]:VEC["c"] + 2 * KT] = both.reshape(2, KT, P).transpose(2, 1, 0).reshape(P, -1)
    vecs[:, VEC["mod_b"]:VEC["mod_b"] + DEPTH * 6 * KT] = np.repeat(a["mod_b"].reshape(-1, P).T, 2, axis=1)
    for name, n in (("pre", "pre_norm"), ("post", "post_norm"), ("qn", "mla_q_norm"), ("kvn", "mla_kv_norm"),
                    ("pscale", "pool_scale"), ("gn", "gla_norm"), ("mixpre", "norm_mix_pre_2"),
                    ("mixpost", "norm_mix_post_2"), ("ffnpre", "norm_ffn_pre_2"), ("ffnpost", "norm_ffn_post_2"),
                    ("convw", "rg_conv_w_2"), ("convb", "rg_conv_b_2"), ("ba", "rg_b_a_2"), ("bi", "rg_b_i_2"),
                    ("lam", "rg_lambda_2")):
        column(name, a[n])
    for l in range(DEPTH):
        column("gab", a["gla_af_b"][l], 4 * l)
        column("gab", a["gla_ab_b"][l], 4 * l + 2)
    vecs[:, VEC["eps"]] = NORM_EPS

    tokens = np.concatenate([a["ctx"][0], a["x"][0]])
    consts, consts2 = constants()
    q, k = np.arange(SEQ).reshape(2, P).T[:, :, None], np.arange(SEQ)[None, None, :]
    arrays = {
        "x_t": np.ascontiguousarray(tokens.reshape(TOK, KT, P).transpose(2, 1, 0)),
        "wstream": ws, "small": small, "vecs": vecs, "consts": consts,
        "rel": np.ascontiguousarray(a["attn_rel_bias_2"][0][:, q - k + SEQ].transpose(1, 0, 2, 3).reshape(P, 2 * HEADS, SEQ)),
        "consts2": consts2,
    }
    nc = bacc.Bacc("TRN2", target_bir_lowering=False, num_devices=1)
    args = [nc.dram_tensor(n, list(x.shape), mybir.dt.float32, kind="ExternalInput").ap() for n, x in arrays.items()]
    out = nc.dram_tensor("out_t", [P, KT, SEQ], mybir.dt.float32, kind="ExternalOutput").ap()
    program(nc, *args, out)
    r = run_bass_kernel_spmd(nc, [arrays], core_ids=[0])
    return np.asarray(r.results[0]["out_t"]).transpose(2, 1, 0).reshape(1, SEQ, D)
```
